# Optimizing a Trainium2 kernel written in Bass

```python
import math
import jax, jax.numpy as jnp
from jax import lax
import numpy as np

D_MODEL = 2048
BATCH = 1
SEQ = 256
DEPTH = 1

RET_HEADS = 8
RET_QK_DIM = 128
RET_V_DIM = 256
RET_QK_WIDTH = RET_HEADS * RET_QK_DIM
RET_V_WIDTH = RET_HEADS * RET_V_DIM
RET_CHUNK = 128
ROPE_BASE = 10000.0
S5_GROUP = 16
S5_WIDTH = D_MODEL // 2
S5_GROUPS = S5_WIDTH // S5_GROUP
S5_STATE = 64
DT_MIN = 1e-3
DT_MAX = 1e-1
D_FF = -(-8 * D_MODEL // (3 * 256)) * 256
NORM_EPS = 1e-6
GN_EPS = 1e-5

IN_SIZES = (RET_QK_WIDTH, RET_QK_WIDTH, RET_V_WIDTH, RET_V_WIDTH, S5_WIDTH, D_MODEL, D_MODEL)
IN_WIDTH = sum(IN_SIZES)
IN_SPLITS = tuple(int(s) for s in np.cumsum(IN_SIZES)[:-1])


def rmsnorm(x, g):
    xf = x.astype(jnp.float32)
    y = xf * lax.rsqrt(jnp.mean(xf * xf, axis=-1, keepdims=True) + NORM_EPS)
    return (y * g.astype(jnp.float32)).astype(x.dtype)

def head_group_norm(y):
    yf = y.astype(jnp.float32)
    mu = jnp.mean(yf, axis=-1, keepdims=True)
    var = jnp.mean(jnp.square(yf - mu), axis=-1, keepdims=True)
    return ((yf - mu) * lax.rsqrt(var + GN_EPS)).astype(y.dtype)

def rope(t, cos, sin):
    t1, t2 = jnp.split(t, 2, axis=-1)
    return jnp.concatenate([t1 * cos - t2 * sin, t1 * sin + t2 * cos], axis=-1)

def retention(q, k, v):
    Bn, L, H, dk = q.shape
    dv = v.shape[-1]
    C = RET_CHUNK
    N = L // C
    dt = q.dtype
    log_g = jnp.log1p(-jnp.exp2(-5.0 - jnp.arange(H, dtype=jnp.float32)))
    idx = jnp.arange(C, dtype=jnp.float32)
    rel = idx[:, None] - idx[None, :]
    decay = jnp.where(rel[None] >= 0,
                      jnp.exp(jnp.maximum(rel, 0.0)[None] * log_g[:, None, None]), 0.0)
    w_state = jnp.exp((C - 1.0 - idx)[:, None] * log_g[None, :])
    w_cross = jnp.exp((idx + 1.0)[:, None] * log_g[None, :])
    chunk_decay = jnp.exp(C * log_g)

    qc = q.reshape(Bn, N, C, H, dk)
    kc = k.reshape(Bn, N, C, H, dk)
    vc = v.reshape(Bn, N, C, H, dv)

    scores = jnp.einsum('bnchd,bnshd->bnhcs', qc, kc) * decay.astype(dt)[None, None]
    inner = jnp.einsum('bnhcs,bnshv->bnchv', scores, vc)

    kv = jnp.einsum('bnchd,ch,bnchv->bnhdv', kc, w_state.astype(dt), vc)
    cd = chunk_decay.astype(dt)[None, :, None, None]

    def step(R, kv_n):
        return cd * R + kv_n, R

    R0 = jnp.zeros((Bn, H, dk, dv), dtype=kv.dtype)
    _, R_prev = lax.scan(step, R0, jnp.moveaxis(kv, 1, 0))
    R_prev = jnp.moveaxis(R_prev, 0, 1)

    cross = jnp.einsum('bnchd,bnhdv->bnchv', qc, R_prev) * w_cross.astype(dt)[None, None, :, :, None]
    return (inner + cross).reshape(Bn, L, H, dv)

def s5_ssm(u, a_re, a_im, log_dt, b_re, b_im, c_re, c_im, d_skip):
    Bn, L, _ = u.shape
    ug = u.reshape(Bn, L, S5_GROUPS, S5_GROUP)
    dt = jnp.exp(log_dt)[:, None]
    mag = jnp.exp(a_re * dt)
    lb_re = mag * jnp.cos(a_im * dt)
    lb_im = mag * jnp.sin(a_im * dt)
    nr = lb_re - 1.0
    den = a_re * a_re + a_im * a_im
    f_re = (nr * a_re + lb_im * a_im) / den
    f_im = (lb_im * a_re - nr * a_im) / den
    bb_re = f_re[..., None] * b_re - f_im[..., None] * b_im
    bb_im = f_re[..., None] * b_im + f_im[..., None] * b_re
    bu_re = jnp.einsum('blgh,gph->blgp', ug, bb_re)
    bu_im = jnp.einsum('blgh,gph->blgp', ug, bb_im)
    A_re = jnp.broadcast_to(lb_re, (L,) + lb_re.shape)
    A_im = jnp.broadcast_to(lb_im, (L,) + lb_im.shape)

    def combine(e1, e2):
        a1r, a1i, b1r, b1i = e1
        a2r, a2i, b2r, b2i = e2
        return (a1r * a2r - a1i * a2i,
                a1r * a2i + a1i * a2r,
                a2r * b1r - a2i * b1i + b2r,
                a2r * b1i + a2i * b1r + b2i)

    def scan_one(br, bi):
        _, _, xr, xi = lax.associative_scan(combine, (A_re, A_im, br, bi), axis=0)
        return xr, xi

    x_re, x_im = jax.vmap(scan_one)(bu_re, bu_im)
    y = (jnp.einsum('blgp,ghp->blgh', x_re, c_re)
         - jnp.einsum('blgp,ghp->blgh', x_im, c_im)
         + d_skip[None, None] * ug)
    return y.reshape(Bn, L, S5_WIDTH)

def token_mixer(h, w_in, w_ret_out, a_re, a_im, log_dt, b_re, b_im, c_re, c_im, d_skip,
                w_s5_glu, w_out, cos, sin):
    Bn, L, _ = h.shape
    proj = h @ w_in
    q, k, v, g_ret, u, gate_r, gate_s = jnp.split(proj, IN_SPLITS, axis=-1)
    q = rope(q.reshape(Bn, L, RET_HEADS, RET_QK_DIM), cos, sin)
    k = rope(k.reshape(Bn, L, RET_HEADS, RET_QK_DIM), cos, sin) * (RET_QK_DIM ** -0.5)
    v = v.reshape(Bn, L, RET_HEADS, RET_V_DIM)
    ret = head_group_norm(retention(q, k, v)).reshape(Bn, L, RET_V_WIDTH)
    y_ret = (jax.nn.silu(g_ret) * ret) @ w_ret_out
    y_ssm = jax.nn.gelu(s5_ssm(u, a_re, a_im, log_dt, b_re, b_im, c_re, c_im, d_skip))
    glu_a, glu_b = jnp.split(y_ssm @ w_s5_glu, 2, axis=-1)
    y_s5 = glu_a * jax.nn.sigmoid(glu_b)
    merged = jax.nn.sigmoid(gate_r) * y_ret + jax.nn.sigmoid(gate_s) * y_s5
    return merged @ w_out

def swiglu_ffn(h, w_ffn_in, w_ffn_out):
    a, b = jnp.split(h @ w_ffn_in, 2, axis=-1)
    return (jax.nn.silu(a) * b) @ w_ffn_out

def first_inputs(seed: int = 0) -> dict:
    key = jax.random.key(seed)
    ks = jax.random.split(key, 20)
    f32 = jnp.float32

    def dense(k, shape, fan_in):
        return jax.random.normal(k, shape, f32) * (fan_in ** -0.5)

    x = jax.random.normal(ks[0], (BATCH, SEQ, D_MODEL), f32)
    c = jax.random.normal(ks[1], (BATCH, D_MODEL), f32)
    w_ada = dense(ks[2], (DEPTH, D_MODEL, 6 * D_MODEL), D_MODEL)
    b_ada = 0.01 * jax.random.normal(ks[3], (DEPTH, 6 * D_MODEL), f32)
    norm_gains = 1.0 + 0.05 * jax.random.normal(ks[4], (DEPTH, 4, D_MODEL), f32)
    w_in = dense(ks[5], (DEPTH, D_MODEL, IN_WIDTH), D_MODEL)
    w_ret_out = dense(ks[6], (DEPTH, RET_V_WIDTH, D_MODEL), RET_V_WIDTH)
    ssm_a_re = -0.5 + 0.01 * jax.random.normal(ks[7], (DEPTH, S5_GROUPS, S5_STATE), f32)
    ssm_a_im = jnp.broadcast_to(math.pi * jnp.arange(S5_STATE, dtype=f32),
                                (DEPTH, S5_GROUPS, S5_STATE))
    ssm_log_dt = jax.random.uniform(ks[8], (DEPTH, S5_GROUPS), f32,
                                    math.log(DT_MIN), math.log(DT_MAX))
    ssm_b_re = dense(ks[9], (DEPTH, S5_GROUPS, S5_STATE, S5_GROUP), 2 * S5_GROUP)
    ssm_b_im = dense(ks[10], (DEPTH, S5_GROUPS, S5_STATE, S5_GROUP), 2 * S5_GROUP)
    ssm_c_re = 0.5 * jax.random.normal(ks[11], (DEPTH, S5_GROUPS, S5_GROUP, S5_STATE), f32)
    ssm_c_im = 0.5 * jax.random.normal(ks[12], (DEPTH, S5_GROUPS, S5_GROUP, S5_STATE), f32)
    ssm_d = jax.random.normal(ks[13], (DEPTH, S5_GROUPS, S5_GROUP), f32)
    w_s5_glu = dense(ks[14], (DEPTH, S5_WIDTH, 2 * D_MODEL), S5_WIDTH)
    w_out = dense(ks[15], (DEPTH, D_MODEL, D_MODEL), D_MODEL)
    w_ffn_in = dense(ks[16], (DEPTH, D_MODEL, 2 * D_FF), D_MODEL)
    w_ffn_out = dense(ks[17], (DEPTH, D_FF, D_MODEL), D_FF)
    return {"x": x, "c": c, "w_ada": w_ada, "b_ada": b_ada, "norm_gains": norm_gains,
            "w_in": w_in, "w_ret_out": w_ret_out, "ssm_a_re": ssm_a_re, "ssm_a_im": ssm_a_im,
            "ssm_log_dt": ssm_log_dt, "ssm_b_re": ssm_b_re, "ssm_b_im": ssm_b_im,
            "ssm_c_re": ssm_c_re, "ssm_c_im": ssm_c_im, "ssm_d": ssm_d, "w_s5_glu": w_s5_glu,
            "w_out": w_out, "w_ffn_in": w_ffn_in, "w_ffn_out": w_ffn_out}

def first_block(x, c, w_ada, b_ada, norm_gains, w_in, w_ret_out, ssm_a_re, ssm_a_im, ssm_log_dt,
              ssm_b_re, ssm_b_im, ssm_c_re, ssm_c_im, ssm_d, w_s5_glu, w_out, w_ffn_in, w_ffn_out):
    L = x.shape[1]
    pos = jnp.arange(L, dtype=jnp.float32)
    inv_freq = ROPE_BASE ** (-jnp.arange(RET_QK_DIM // 2, dtype=jnp.float32) * (2.0 / RET_QK_DIM))
    ang = pos[:, None] * inv_freq[None, :]
    cos = jnp.cos(ang)[None, :, None, :].astype(x.dtype)
    sin = jnp.sin(ang)[None, :, None, :].astype(x.dtype)
    c_act = jax.nn.silu(c)
    for l in range(DEPTH):
        mod = c_act @ w_ada[l] + b_ada[l]
        sh_m, sc_m, gt_m, sh_f, sc_f, gt_f = [m[:, None, :] for m in jnp.split(mod, 6, axis=-1)]
        g = norm_gains[l]
        h = rmsnorm(x, g[0]) * (1.0 + sc_m) + sh_m
        y = token_mixer(h, w_in[l], w_ret_out[l], ssm_a_re[l], ssm_a_im[l], ssm_log_dt[l],
                        ssm_b_re[l], ssm_b_im[l], ssm_c_re[l], ssm_c_im[l], ssm_d[l],
                        w_s5_glu[l], w_out[l], cos, sin)
        x = x + gt_m * rmsnorm(y, g[1])
        h = rmsnorm(x, g[2]) * (1.0 + sc_f) + sh_f
        y = swiglu_ffn(h, w_ffn_in[l], w_ffn_out[l])
        x = x + gt_f * rmsnorm(y, g[3])
    return x


BRANCH_WIDTH = D_MODEL // 2
N_BRANCH = 3
ATTN_HEAD_DIM = 128
ATTN_HEADS = BRANCH_WIDTH // ATTN_HEAD_DIM
ATTN_WIDTH = ATTN_HEADS * ATTN_HEAD_DIM
MOBA_BLOCK = 256
MOBA_TOPK = 3
QUERY_CHUNK = 64
GLA_HEADS = 4
GLA_VAL_DIM = BRANCH_WIDTH // GLA_HEADS
GLA_KEY_DIM = GLA_VAL_DIM // 2
GLA_KEY_WIDTH = GLA_HEADS * GLA_KEY_DIM
GLA_VAL_WIDTH = GLA_HEADS * GLA_VAL_DIM
GLA_GATE_RANK = 16
GLA_GATE_TAU = 16.0
GLA_CHUNK = 64
CONV_WIDTH = BRANCH_WIDTH
CONV_K = 3
D_FF_2 = -(-8 * D_MODEL // (3 * 256)) * 256
RMS_EPS = 1e-6
COL_SIZES = (ATTN_WIDTH, ATTN_WIDTH, ATTN_WIDTH,
             GLA_KEY_WIDTH, GLA_KEY_WIDTH, GLA_VAL_WIDTH,
             GLA_VAL_WIDTH, GLA_GATE_RANK,
             CONV_WIDTH, CONV_WIDTH, CONV_WIDTH,
             N_BRANCH * D_MODEL)
N_IN_COLS = sum(COL_SIZES)


def rms_norm(x, w):
    xf = x.astype(jnp.float32)
    y = xf * lax.rsqrt(jnp.mean(xf * xf, axis=-1, keepdims=True) + RMS_EPS)
    return (y * w.astype(jnp.float32)).astype(x.dtype)

def moba_attention(q, k, v):
    B_, S, H, dh = q.shape
    f32 = jnp.float32
    nb = -(-S // MOBA_BLOCK)
    s_pad = nb * MOBA_BLOCK
    topk = min(MOBA_TOPK, nb)
    pad = ((0, 0), (0, s_pad - S), (0, 0), (0, 0))
    kp = jnp.pad(k, pad)
    vp = jnp.pad(v, pad)
    kb = kp.reshape(B_, nb, MOBA_BLOCK, H, dh).transpose(0, 3, 1, 2, 4)
    vb = vp.reshape(B_, nb, MOBA_BLOCK, H, dh).transpose(0, 3, 1, 2, 4)
    k_mean = jnp.mean(kb.astype(f32), axis=3)
    slopes = 2.0 ** (-8.0 * jnp.arange(1, H + 1, dtype=f32) / H)
    scale = 1.0 / math.sqrt(dh)
    bi = jnp.arange(B_)[:, None, None, None]
    hi = jnp.arange(H)[None, None, :, None]
    blk_ids = jnp.arange(nb)
    in_blk = jnp.arange(MOBA_BLOCK)

    def one_chunk(c):
        start = c * QUERY_CHUNK
        qf = lax.dynamic_slice_in_dim(q, start, QUERY_CHUNK, axis=1).astype(f32)
        t_pos = start + jnp.arange(QUERY_CHUNK)
        own = start // MOBA_BLOCK
        gate = jnp.einsum("bqhd,bhnd->bqhn", qf, k_mean)
        gate = jnp.where((blk_ids < own)[None, None, None, :], gate, -jnp.inf)
        _, sel = lax.top_k(gate, topk)
        sel_valid = sel < own
        k_sel = kb[bi, hi, sel].astype(f32)
        v_sel = vb[bi, hi, sel].astype(f32)
        s_sel = jnp.einsum("bqhd,bqhnkd->bqhnk", qf, k_sel) * scale
        kpos_sel = sel[..., None] * MOBA_BLOCK + in_blk
        dist_sel = (t_pos[None, :, None, None, None] - kpos_sel).astype(f32)
        s_sel = s_sel - slopes[None, None, :, None, None] * dist_sel
        s_sel = jnp.where(sel_valid[..., None], s_sel, -jnp.inf)
        k_own = lax.dynamic_slice_in_dim(kp, own * MOBA_BLOCK, MOBA_BLOCK, axis=1).astype(f32)
        v_own = lax.dynamic_slice_in_dim(vp, own * MOBA_BLOCK, MOBA_BLOCK, axis=1).astype(f32)
        s_own = jnp.einsum("bqhd,bkhd->bqhk", qf, k_own) * scale
        dist_own = t_pos[:, None] - (own * MOBA_BLOCK + in_blk)[None, :]
        s_own = s_own - slopes[None, None, :, None] * dist_own[None, :, None, :].astype(f32)
        s_own = jnp.where((dist_own >= 0)[None, :, None, :], s_own, -jnp.inf)
        n_sel = topk * MOBA_BLOCK
        p = jax.nn.softmax(jnp.concatenate(
            [s_sel.reshape(B_, QUERY_CHUNK, H, n_sel), s_own], axis=-1), axis=-1)
        p_sel = p[..., :n_sel].reshape(B_, QUERY_CHUNK, H, topk, MOBA_BLOCK)
        out = (jnp.einsum("bqhnk,bqhnkd->bqhd", p_sel, v_sel)
               + jnp.einsum("bqhk,bkhd->bqhd", p[..., n_sel:], v_own))
        return out.astype(q.dtype)

    outs = lax.map(one_chunk, jnp.arange(S // QUERY_CHUNK))
    return outs.transpose(1, 0, 2, 3, 4).reshape(B_, S, H, dh)

def gla_attention(q, k, v, log_a):
    B_, S, H, dk = q.shape
    dv = v.shape[-1]
    f32 = jnp.float32
    n = S // GLA_CHUNK

    def chunked(t):
        return t.astype(f32).reshape(B_, n, GLA_CHUNK, H, t.shape[-1]).transpose(0, 3, 1, 2, 4)

    qc = chunked(q) * (dk ** -0.5)
    kc, vc = chunked(k), chunked(v)
    b = jnp.cumsum(chunked(log_a), axis=3)
    b_last = b[..., -1:, :]
    q_in = qc * jnp.exp(b)
    k_in = kc * jnp.exp(-b)
    k_dec = kc * jnp.exp(b_last - b)
    causal = jnp.tril(jnp.ones((GLA_CHUNK, GLA_CHUNK), dtype=bool))
    a_intra = jnp.where(causal, jnp.einsum("bhncd,bhnsd->bhncs", q_in, k_in), 0.0)
    o_intra = jnp.einsum("bhncs,bhnse->bhnce", a_intra, vc)
    kv = jnp.einsum("bhncd,bhnce->bhnde", k_dec, vc)
    decay = jnp.exp(b_last[..., 0, :])

    def step(state, inp):
        kv_n, d_n = inp
        return d_n[..., None] * state + kv_n, state

    _, s_prev = lax.scan(step, jnp.zeros((B_, H, dk, dv), f32),
                         (kv.transpose(2, 0, 1, 3, 4), decay.transpose(2, 0, 1, 3)))
    s_prev = s_prev.transpose(1, 2, 0, 3, 4)
    o = o_intra + jnp.einsum("bhncd,bhnde->bhnce", q_in, s_prev)
    return o.transpose(0, 2, 3, 1, 4).reshape(B_, S, H, dv)

def short_conv(u, w):
    ch = u.shape[-1]
    return lax.conv_general_dilated(
        u, w[:, None, :].astype(u.dtype), window_strides=(1,), padding=[(CONV_K - 1, 0)],
        dimension_numbers=("NWC", "WIO", "NWC"), feature_group_count=ch)

def second_inputs(seed: int = 0) -> dict:
    key = jax.random.key(seed)
    ks = jax.random.split(key, 16)
    L, D = DEPTH, D_MODEL
    nrm = lambda k, shape, s: jax.random.normal(k, shape, jnp.float32) * s
    gain = lambda k, shape: 1.0 + 0.02 * jax.random.normal(k, shape, jnp.float32)
    return {
        "x": nrm(ks[0], (BATCH, SEQ, D), 1.0),
        "norm1_w": gain(ks[1], (L, D)),
        "w_in": nrm(ks[2], (L, D, N_IN_COLS), D ** -0.5),
        "gla_w_up": nrm(ks[3], (L, GLA_GATE_RANK, GLA_KEY_WIDTH), GLA_GATE_RANK ** -0.5),
        "gla_b": nrm(ks[4], (L, GLA_KEY_WIDTH), 0.02),
        "gla_norm_w": gain(ks[5], (L, GLA_VAL_DIM)),
        "conv_w": nrm(ks[6], (L, CONV_K, CONV_WIDTH), CONV_K ** -0.5),
        "w_br_attn": nrm(ks[7], (L, ATTN_WIDTH, D), ATTN_WIDTH ** -0.5),
        "w_br_gla": nrm(ks[8], (L, GLA_VAL_WIDTH, D), GLA_VAL_WIDTH ** -0.5),
        "w_br_conv": nrm(ks[9], (L, CONV_WIDTH, D), CONV_WIDTH ** -0.5),
        "w_out": nrm(ks[10], (L, D, D), D ** -0.5),
        "norm2_w": gain(ks[11], (L, D)),
        "w_ffn_gate": nrm(ks[12], (L, D, D_FF_2), D ** -0.5),
        "w_ffn_up": nrm(ks[13], (L, D, D_FF_2), D ** -0.5),
        "w_ffn_down": nrm(ks[14], (L, D_FF_2, D), D_FF_2 ** -0.5),
        "final_norm_w": gain(ks[15], (D,)),
    }

def second_block(x, norm1_w, w_in, gla_w_up, gla_b, gla_norm_w, conv_w, w_br_attn, w_br_gla,
              w_br_conv, w_out, norm2_w, w_ffn_gate, w_ffn_up, w_ffn_down, final_norm_w):
    B_, S, D = x.shape
    f32 = jnp.float32
    splits = [int(s) for s in np.cumsum(COL_SIZES)[:-1]]
    for l in range(DEPTH):
        h = rms_norm(x, norm1_w[l])
        proj = h @ w_in[l]
        (q_a, k_a, v_a, q_g, k_g, v_g, r_g, a_down,
         b_gate, c_gate, u_conv, merge) = jnp.split(proj, splits, axis=-1)
        hs_a = (B_, S, ATTN_HEADS, ATTN_HEAD_DIM)
        o_a = moba_attention(q_a.reshape(hs_a), k_a.reshape(hs_a), v_a.reshape(hs_a))
        br_a = o_a.reshape(B_, S, ATTN_WIDTH) @ w_br_attn[l]
        z = (a_down @ gla_w_up[l]).astype(f32) + gla_b[l].astype(f32)
        log_a = jax.nn.log_sigmoid(z) / GLA_GATE_TAU
        hs_k = (B_, S, GLA_HEADS, GLA_KEY_DIM)
        o_g = gla_attention(q_g.reshape(hs_k), k_g.reshape(hs_k),
                            v_g.reshape(B_, S, GLA_HEADS, GLA_VAL_DIM), log_a.reshape(hs_k))
        o_g = o_g * lax.rsqrt(jnp.mean(o_g * o_g, axis=-1, keepdims=True) + RMS_EPS)
        o_g = o_g * gla_norm_w[l].astype(f32)
        o_g = o_g.reshape(B_, S, GLA_VAL_WIDTH) * jax.nn.silu(r_g.astype(f32))
        br_b = o_g.astype(x.dtype) @ w_br_gla[l]
        y_c = b_gate * short_conv(c_gate * u_conv, conv_w[l])
        br_c = y_c @ w_br_conv[l]
        g = jax.nn.sigmoid(merge.astype(f32)).reshape(B_, S, N_BRANCH, D)
        mixed = (g[:, :, 0] * br_a.astype(f32) + g[:, :, 1] * br_b.astype(f32)
                 + g[:, :, 2] * br_c.astype(f32)).astype(x.dtype)
        x = x + mixed @ w_out[l]
        h2 = rms_norm(x, norm2_w[l])
        x = x + (jax.nn.silu(h2 @ w_ffn_gate[l]) * (h2 @ w_ffn_up[l])) @ w_ffn_down[l]
    return rms_norm(x, final_norm_w)


def setup_inputs(seed=0):
    out = dict(first_inputs(seed))
    for name, value in second_inputs(seed + 1).items():
        if name != "x":
            out[name + "_2"] = value
    return out


def reference(
    x, c, w_ada, b_ada, norm_gains, w_in, w_ret_out, ssm_a_re, ssm_a_im, ssm_log_dt, ssm_b_re,
    ssm_b_im, ssm_c_re, ssm_c_im, ssm_d, w_s5_glu, w_out, w_ffn_in, w_ffn_out, norm1_w_2,
    w_in_2, gla_w_up_2, gla_b_2, gla_norm_w_2, conv_w_2, w_br_attn_2, w_br_gla_2, w_br_conv_2,
    w_out_2, norm2_w_2, w_ffn_gate_2, w_ffn_up_2, w_ffn_down_2, final_norm_w_2,
):
    x = first_block(
        x, c, w_ada, b_ada, norm_gains, w_in, w_ret_out, ssm_a_re, ssm_a_im, ssm_log_dt,
        ssm_b_re, ssm_b_im, ssm_c_re, ssm_c_im, ssm_d, w_s5_glu, w_out, w_ffn_in, w_ffn_out,
    )
    return second_block(
        x, norm1_w_2, w_in_2, gla_w_up_2, gla_b_2, gla_norm_w_2, conv_w_2, w_br_attn_2,
        w_br_gla_2, w_br_conv_2, w_out_2, norm2_w_2, w_ffn_gate_2, w_ffn_up_2, w_ffn_down_2,
        final_norm_w_2,
    )


_drawn_inputs = setup_inputs


def setup_inputs(seed=0):
    import zlib

    import numpy as np

    out = dict(_drawn_inputs(seed))
    spreads = {}
    factors = {'ssm_a_re': 64.0,
     'norm1_w_2': 3.236,
     'gla_b_2': 8.0,
     'gla_norm_w_2': 40.344,
     'norm2_w_2': 16.528,
     'final_norm_w_2': 8.537}
    for name, (base, spread) in spreads.items():
        noise = np.random.default_rng([zlib.crc32(name.encode()), seed]).standard_normal(out[name].shape)
        drawn = base * np.exp(spread * noise) if base else spread * noise
        out[name] = __import__('jax').numpy.asarray(drawn.astype(out[name].dtype))
    for name, factor in factors.items():
        out[name] = (out[name] * factor).astype(out[name].dtype)
    return out
```

```python
from contextlib import ExitStack

import concourse.bass as bass
from concourse import mybir

F32 = mybir.dt.float32
F32R = mybir.dt.float32r
I32 = mybir.dt.int32
ALU = mybir.AluOpType
ACT = mybir.ActivationFunctionType
AX_X = mybir.AxisListType.X

P = 128
T = 256
D = 2048
KT = D // P
HALF = 1024 // P
FF = 5632 // P
HEADS = 8
GLA_HEADS = 4
V_DIM = 256
RANK = 16
GLA_CHUNKS = 4
S5_TILES = 32
LEVELS = 8
NORM_EPS = 1e-6
GN_EPS = 1e-5
QK_SCALE = 128.0 ** -0.5
GLA_TAU = 16.0
GELU_IN = (2.0 / 3.141592653589793) ** 0.5
GELU_CUBE = 0.044715
TURN_HI = 6.28125
TURN_LO = 0.0019353071795864769
TURN = TURN_HI + TURN_LO
PI_IN = 3.1415925
ROUND = 1.5 * 2.0 ** 23
SLOTS = 4
W, ADA = "w", "ada"


class Phase:

    def __init__(self, iters, blocks, outs, summed=False, beside=1):
        self.iters, self.blocks, self.outs, self.summed, self.beside = iters, blocks, outs, summed, beside
        self.opens = False
        self.tiles = [n for kind, n in blocks if kind == W]
        self.asides = len(blocks) - len(self.tiles)
        assert len(self.tiles) % SLOTS == 0 and outs % 2 == 0
        self.offsets = [sum(n for _, n in blocks[:j]) * P * P for j in range(len(blocks))]
        self.words = sum(n for _, n in blocks) * P * P

    def uses(self, g, m):
        return g * (len(self.tiles) // SLOTS) + (self.first_block // SLOTS + m // SLOTS + 1)

    def weight_count(self, g, m):
        return g * len(self.tiles) + (self.first_weight + m + 1)

    def out_count(self, g, o):
        return g * self.outs + (self.first_out + o + 1)

    def asides_in(self, k):
        return len(range(k, self.asides, self.beside))

    def aside_count(self, g, i):
        k = i % self.beside
        return g * self.asides_in(k) + (self.first_aside[k] + i // self.beside + 1)

    def tiles_of(self, m):
        return self.tiles[m] if m < len(self.tiles) else KT


def schedule():
    w = (W, KT)
    a = (ADA, KT)
    ph = {
        "ada": Phase(8, [w] * 4, 0, summed=True),
        "u": Phase(2, [w] * 4 + [a] * 2, 4, beside=2),
        "heads": Phase(4, [w, w, w, a, w, w, a, w, w, w, a, w, w, a, w, w, a], 12),
        "ret": Phase(4, [w] * 8, 8),
        "glu": Phase(4, [w, w, a] * 4, 12, beside=2),
        "out1": Phase(4, [w, w, a, w, w, a], 4, beside=2),
        "ffa": Phase(4, [w, w, w, w, a, w, w, a, w, w, a, a], 8, beside=2),
        "ffb": Phase(7, [w] * 8, 8),
        "down1": Phase(4, [w, w, (W, 12)] * 4, 4),
        "att": Phase(2, [w] * 12, 12),
        "gla": Phase(2, [w] * 12, 12),
        "conv": Phase(2, [w] * 12, 12),
        "mrg0": Phase(4, [w] * 4, 4),
        "mix": Phase(8, [w, w, w, (W, 8)] * 2, 10),
        "out2": Phase(4, [w] * 4, 4),
        "ff2": Phase(11, [w] * 8, 8),
        "down2": Phase(4, [w, w, (W, 12)] * 4, 4),
    }
    for name in ("u", "ffa", "att", "ff2"):
        ph[name].opens = True
    block = weight = out = 0
    aside = [0, 0]
    for p in ph.values():
        p.first_block, p.first_weight, p.first_out, p.first_aside = block, weight, out, list(aside)
        block += p.iters * len(p.tiles)
        weight += p.iters * len(p.tiles) * (not p.summed)
        out += p.iters * p.outs
        for k in range(p.beside):
            aside[k] += p.iters * p.asides_in(k)
    return ph


def one(n):
    return bass.ds(n, 1)


class Own:

    def __init__(self, eng, sem):
        self.eng, self.sem, self.base, self.per, self.g, self.k, self.shift = eng, sem, 0, 0, 0, 0, 0

    def enter(self, per, g, first=0):
        self.per, self.k = per, 0
        self.g, self.shift = (0, 0) if isinstance(g, int) else (g, first * per)

    def leave(self, times=1):
        assert self.k == self.per, f"{self.k} own steps, {self.per} were stated"
        self.base += self.per * times
        self.per = self.g = self.k = self.shift = 0

    def mark(self, ins):
        ins.then_inc(self.sem, 1)
        self.k += 1
        return self.g * self.per + (self.base + self.k - self.shift)

    def step(self, ins):
        self.eng.wait_ge(self.sem, self.mark(ins))
        if not self.per:
            self.leave_straight()

    def leave_straight(self):
        self.base, self.k = self.base + self.k, 0




def program(nc, dram, out):
    ph = schedule()
    with ExitStack() as ctx:
        def sb(stack, name, shape, dt=F32):
            return stack.enter_context(nc.sbuf_tensor(name, shape, dt))

        def sem(name):
            return ctx.enter_context(nc.semaphore(name))

        raw, hi, lo = [], [], []
        for s in range(SLOTS):
            with ExitStack() as shared:
                raw.append(sb(shared, f"ring_raw{s}", [P, KT, P]))
            lo.append(sb(ctx, f"ring_lo{s}", [P, KT, P], F32R))
            hi.append(sb(ctx, f"ring_hi{s}", [P, KT, P], F32R))
        x = sb(ctx, "x_res", [P, KT, T])
        half = [sb(ctx, f"half{i}", [P, T]) for i in range(2)]
        ident = sb(ctx, "ident", [P, P])
        ones = sb(ctx, "ones", [P, P])
        gains = sb(ctx, "gains_sb", [P, 7, KT])
        mod = sb(ctx, "mod", [P, 96])
        b_ada = sb(ctx, "b_ada_sb", [P, 96])
        gain = sb(ctx, "gain", [P, 4, KT])
        ada_sum = sb(ctx, "ada_sum", [P, 6])
        sq_sum = sb(ctx, "sq_sum", [P, T])
        rstd = sb(ctx, "rstd", [P, T])
        tile = [sb(ctx, f"tile{i}", [P, T]) for i in range(2)]
        eps = sb(ctx, "eps", [P, 2])

        with ExitStack() as shared:
            y2 = sb(shared, "y2", [P, KT, T])
        with ExitStack() as shared:
            normed = sb(shared, "normed", [P, KT, 2 * T])
        h = sb(ctx, "h_split", [P, KT, 2 * T], F32R)

        with ExitStack() as block1:
            c_act = sb(block1, "c_act", [P, D])
            with ExitStack() as mixer:
                rope = sb(mixer, "rope_sb", [P, 2, T])
                lag = sb(mixer, "lag_sb", [P, T])
                log_g = sb(mixer, "log_g_sb", [P, HEADS])
                with ExitStack() as shared:
                    sb(shared, "ret_first", [P, HEADS - 2, 2, 2 * T])
                    aside_r = sb(shared, "aside_r", [P, D])
                with ExitStack() as shared:
                    ret = sb(shared, "ret_split", [P, HEADS, 2, 2 * T], F32R)
                merged = sb(mixer, "merged_split", [P, KT, 2 * T], F32R)
                with ExitStack() as shared:
                    sb(shared, "y_ssm_first", [P, HALF // 2, 2 * T])
                    aside_y = sb(shared, "aside_y", [P, D])
                y_ssm = sb(mixer, "y_ssm_split", [P, HALF, 2 * T], F32R)
                with ExitStack() as shared:
                    aside_u = sb(shared, "aside_u", [P, D])
                u = sb(mixer, "u", [P, HALF, T])
                s5_a = sb(mixer, "s5_a_sb", [P, 3, S5_TILES])
                s5_d = sb(mixer, "s5_d_sb", [P, HALF])
                s5_p = sb(mixer, "s5_p", [P, S5_TILES, 4 * LEVELS + 3])
                with ExitStack() as shared:
                    aside_s = sb(shared, "aside_s", [P, D])
                s5_now = [sb(mixer, f"s5_now{i}", [P, 4 * LEVELS + 3]) for i in range(2)]
                s5_b = [sb(mixer, f"s5_b_sb{i}", [P, 2, P]) for i in range(2)]
                s5_c = [sb(mixer, f"s5_c_sb{i}", [P, 2, P]) for i in range(2)]
                s5_prod = sb(mixer, "s5_prod", [P, 2, 2, T // 4])
                s5_x = [sb(mixer, f"s5_x{i}", [P, 2, T]) for i in range(2)]
                s5_y = sb(mixer, "s5_y", [P, T])
                s5_g = sb(mixer, "s5_g", [P, T])
                with ExitStack() as retention:
                    qk = sb(retention, "qk", [P, 2, T])
                    qk_sin = sb(retention, "qk_sin", [P, 2, T])
                    qk_rot = sb(retention, "qk_rot", [P, 2, T])
                    v_t = sb(retention, "v_t", [P, 2, T])
                    v_n = sb(retention, "v_n", [P, 2, T])
                    g_t = sb(retention, "g_t", [P, 2, T])
                    g_act = sb(retention, "g_act", [P, 2, T])
                    scores = sb(retention, "scores", [P, 384])
                    o_t = sb(retention, "o_t", [P, 2, T])
                    std = sb(retention, "std", [P, T])
                with ExitStack() as after:
                    m_ret = sb(after, "m_ret", [P, KT, T])
                    gate = sb(after, "gate", [P, T])
                    val_a = sb(after, "val_a", [P, T])
                    val_b = sb(after, "val_b", [P, T])
                with ExitStack() as before:
                    c_tanh_half = sb(before, "c_tanh_half", [P, D])
                    s5_t = sb(before, "s5_t", [P, 12, S5_TILES])
                with ExitStack() as after:
                    y1 = sb(after, "y1", [P, KT, T])
            with ExitStack() as ffn:
                with ExitStack() as shared:
                    sb(shared, "ffn1_first", [P, FF - 8, 2 * T])
                    aside_f = [sb(shared, f"aside_f{k}", [P, D]) for k in range(2)]
                f1 = sb(ffn, "ffn1_split", [P, FF, 2 * T], F32R)
                f1_a = [sb(ffn, f"ffn1_a{i}", [P, T]) for i in range(2)]
                f1_b = [sb(ffn, f"ffn1_b{i}", [P, T]) for i in range(2)]
                f1_t = [sb(ffn, f"ffn1_t{i}", [P, T]) for i in range(2)]

        with ExitStack() as block2:
            with ExitStack() as mixer:
                o_att = sb(mixer, "o_att_split", [P, HEADS, 2 * T], F32R)
                o_gla = sb(mixer, "o_gla_split", [P, GLA_HEADS, 2, 2 * T], F32R)
                with ExitStack() as early:
                    ago = sb(early, "ago_sb", [P, 2, T])
                    slopes = sb(early, "slopes_sb", [P, HEADS])
                    causal = sb(early, "causal_sb", [P, 2, P], I32)
                    carry = sb(early, "carry_sb", [P, T])
                    gla_up = sb(early, "gla_up_sb", [RANK, 512])
                    gla_b = sb(early, "gla_b_sb", [P, GLA_HEADS])
                    gla_norm = sb(early, "gla_norm_sb", [P, 2])
                    gla_ad = sb(early, "gla_ad", [RANK, T])
                    ex = sb(early, "ex", [P, 2, T])
                    pre = sb(early, "pre", [P, 2, T])
                    ex_t = sb(early, "ex_t", [P, 384])
                    av_n = sb(early, "av_n", [P, 2, P])
                    sm = sb(early, "sm", [P, 4, 2])
                    a_last = sb(early, "a_last", [P, GLA_HEADS, GLA_CHUNKS])
                y_conv = sb(mixer, "y_conv_split", [P, HALF, 2 * T], F32R)
                with ExitStack() as early:
                    log_a = sb(early, "log_a", [P, GLA_HEADS, T])
                    a_in = sb(early, "a_in", [P, GLA_HEADS, T])
                    a_out = sb(early, "a_out", [P, GLA_HEADS, T])
                    a_end = sb(early, "a_end", [P, GLA_HEADS, T])
                t0 = sb(mixer, "merge0", [P, KT, T])
                conv_w = sb(mixer, "conv_w_sb", [P, HALF, 3])
                with ExitStack() as early:
                    att_q = [sb(early, f"att_q{i}", [P, T]) for i in range(2)]
                    att_k = [sb(early, f"att_k{i}", [P, T]) for i in range(2)]
                    att_v = [sb(early, f"att_v{i}", [P, T]) for i in range(2)]
                    with ExitStack() as first:
                        with ExitStack() as shared:
                            wa_raw = sb(shared, "wa_raw", [P, KT, RANK])
                        wa_lo = sb(first, "wa_lo", [P, KT, RANK], F32R)
                        wa_hi = sb(first, "wa_hi", [P, KT, RANK], F32R)
                    gq = sb(early, "gq", [P, T])
                    gk = sb(early, "gk", [P, T])
                    gv_t = sb(early, "gv_t", [P, 2, T])
                    gr_t = sb(early, "gr_t", [P, 2, T])
                    gr_act = sb(early, "gr_act", [P, 2, T])
                    q_in = [sb(early, f"q_in{i}", [P, T]) for i in range(2)]
                    k_in = sb(early, "k_in", [P, T])
                    k_dec = sb(early, "k_dec", [P, T])
                    gv_n = sb(early, "gv_n", [P, 2, T])
                    k_dec_n = sb(early, "k_dec_n", [P, 3, P])
                    intra = sb(early, "intra", [P, 2, P])
                    state = [sb(early, f"state{i}", [P, T]) for i in range(3)]
                    go = sb(early, "go", [P, 2, T])
                    go_sq = sb(early, "go_sq", [P, 2, T])
                    go_std = sb(early, "go_std", [P, T])
                    go_rstd = sb(early, "go_rstd", [P, T])
                with ExitStack() as late:
                    mixed = sb(late, "mixed_split", [P, KT, 2 * T], F32R)
                    with ExitStack() as conv:
                        cb = sb(conv, "conv_b", [P, T])
                        cc = sb(conv, "conv_c", [P, T])
                        cu = sb(conv, "conv_u", [P, T])
                        cp = sb(conv, "conv_p", [P, T + 2])
                        cy = sb(conv, "conv_y", [P, T])
                    mg = [sb(late, f"mg{i}", [P, T]) for i in range(2)]
                    br = [sb(late, f"br{i}", [P, T]) for i in range(3)]
                    y_out = sb(late, "y_out", [P, T])
            with ExitStack() as ffn:
                f2 = sb(ffn, "ffn2_split", [P, FF, 2 * T], F32R)
                f2_a = [sb(ffn, f"ffn2_a{i}", [P, T]) for i in range(2)]
                f2_b = [sb(ffn, f"ffn2_b{i}", [P, T]) for i in range(2)]
                f2_t = [sb(ffn, f"ffn2_t{i}", [P, T]) for i in range(2)]
                y_down = sb(ffn, "y_down", [P, T])

        def bank(name):
            return ctx.enter_context(nc.psum_tensor(name, [P, 2 * T], F32))

        acc = [bank("acc0"), bank("acc1")]
        p_turn, p_score, p_o, p_norm, p_z, p_y = (bank(n) for n in ("p_turn", "p_score", "p_o", "p_norm", "p_z", "p_y"))

        raw_in = [sem(f"raw_in{s}") for s in range(SLOTS)]
        slot_free = [sem(f"slot_free{s}") for s in range(SLOTS)]
        hi_done, lo_done = sem("hi_done"), sem("lo_done")
        half_done, evac_done = sem("half_done"), sem("evac_done")
        c_in, x_in, start_in, late_in = sem("c_in"), sem("x_in"), sem("start_in"), sem("late_in")
        ones_set, part_done = sem("ones_set"), sem("part_done")
        c_tanh, c_done = sem("c_tanh"), sem("c_done")
        sq_done, sums_done, std_done = sem("sq_done"), sem("sums_done"), sem("std_done")
        sq_used = sem("sq_used")
        n_done, n_hi, h_done = sem("n_done"), sem("n_hi"), sem("h_done")
        dve_own, act_own, pool_own = sem("dve_own"), sem("act_own"), sem("pool_own")
        s5_trig, s5_params = sem("s5_trig"), sem("s5_params")
        s5_b_in = [sem(f"s5_b_in{i}") for i in range(2)]
        s5_c_in = [sem(f"s5_c_in{i}") for i in range(2)]
        z_done, x_half, x_ready = sem("z_done"), sem("x_half"), sem("x_ready")
        scan_core, scan_done, y_part = sem("scan_core"), sem("scan_done"), sem("y_part")
        s5_y_done, s5_sq, s5_in, s5_tanh, s5_m, s5_hi, s5_done = (
            sem(n) for n in ("s5_y_done", "s5_sq", "s5_in", "s5_tanh", "s5_m", "s5_hi", "s5_done"))
        R = {n: sem("ret_" + n) for n in ("rope", "decay", "turned", "scored", "v_n", "masked", "summed", "o", "mean",
                                          "dev", "sq", "var", "std", "tanh", "out", "hi", "done")}
        A = {n: sem("att_" + n) for n in ("turned", "scored", "v_n", "max", "exp", "p", "p_turned", "p_t", "summed",
                                          "hi", "done")}
        B = {n: sem("gla_" + n) for n in ("qk", "turned", "scored", "v_n", "intra", "kv", "s1", "states", "summed", "o",
                                          "var", "std", "tanh", "out", "hi", "done")}
        B0 = {n: sem("gate_" + n) for n in ("hi", "lo", "down", "half", "ad", "z", "zb", "abs", "ln", "log", "cum", "decays", "norm", "zero")}
        gr_tanh, gs_tanh, gb_tanh, mm_done, mm_hi, mm_split = (
            sem(n) for n in ("gr_tanh", "gs_tanh", "gb_tanh", "mm_done", "mm_hi", "mm_split"))
        m_done = sem("m_done")
        f_tanh, f_done, f_hi, f_split = sem("f_tanh"), sem("f_done"), sem("f_hi"), sem("f_split")
        cv_done, cv_hi, cv_split = sem("cv_done"), sem("cv_hi"), sem("cv_split")
        t0_done, mt_done, mx_done, mx_hi, mx_split = (sem(n) for n in ("t0_done", "mt_done", "mx_done", "mx_hi", "mx_split"))
        y_done = sem("y_done")
        out_ready, out_sent = sem("out_ready"), sem("out_sent")

        aside_in, aside_free = [[sem(f"aside_{n}{k}") for k in range(2)] for n in ("in", "free")]
        aside = {"u": [aside_y, aside_r], "heads": [aside_y], "glu": [aside_u, aside_s], "out1": [aside_u, aside_s], "ffa": aside_f}
        BY_POOL = {"glu": (0, 1), "out1": (1,), "ffa": (1,)}
        aside_mul, mod_done = [sem("aside_mul0"), sem("aside_mul1")], sem("mod_done")
        aside_after = {"glu": (s5_done, HALF), "ffa": (y_done, KT)}

        BY_PE = (0, 2, 4)

        block = ctx.enter_context(nc.Block())

        def opening(g):
            return isinstance(g, int) and g == 0

        def bodies(eng, p, first=0, last=0):
            for g in range(first):
                yield g
            if p.iters - last == first + 1:
                yield first
            elif p.iters - last > first:
                with eng.Fori(first, p.iters - last) as g:
                    yield g
            for g in range(p.iters - last, p.iters):
                yield g

        S5_Z = [0, 2, 4, 6]
        S5_Y = [4, 6, 8, 10]
        S5_FIRST = {"heads": 0, "ret": 4}
        S5_TAIL = [m - len(ph["ret"].tiles) for m in S5_Y if m >= len(ph["ret"].tiles)]

        def s5_due(name, g, m, lead=0):
            n = len(ph[name].tiles)
            due = []
            for i, at in enumerate(S5_Y):
                back = (at - lead) // n
                if (at - lead) % n == m and not (back and opening(g)):
                    due.append((i, 4 * (S5_FIRST[name] - back) + i))
            return due

        ret_flat = ret[:].rearrange("p h j c -> p (h j) c")
        gla_flat = o_gla[:].rearrange("p h j c -> p (h j) c")

        def pool_count(name, g, i):
            before = {"glu": (0, 0), "out1": (0, 8), "ffa": (0, 12)}[name]
            return ph[name].asides_in(i % 2) * g + (before[i % 2] + i // 2 + 1)

        @block.sync
        def _(sp):
            sp.dma_start(c_act[:], dram["c_rows"]).then_inc(c_in, 16)
            for name, p in ph.items():
                for g in bodies(sp, p, first=name == "ada"):
                    m = i = 0
                    for (kind, n), offset in zip(p.blocks, p.offsets):
                        src = dram["w_" + name][g, offset:offset + n * P * P].rearrange("(p c) -> p c", p=P)
                        if kind == W:
                            if not (p.summed and isinstance(g, int)):
                                sp.wait_ge(slot_free[m % SLOTS], p.uses(g, m) - 1)
                            sp.dma_start(raw[m % SLOTS][:, 0:n, :].rearrange("p k c -> p (k c)"),
                                         src).then_inc(raw_in[m % SLOTS], 16)
                            m += 1
                        else:
                            count = p.aside_count(g, i)
                            if name in aside_after:
                                sp.wait_ge(*aside_after[name])
                            k = i % p.beside
                            if not isinstance(count, int) or count > 1:
                                sp.wait_ge(aside_free[k], count - 1)
                            sp.dma_start(aside[name][k][:], src).then_inc(aside_in[k], 16)
                            i += 1
            for kt in range(0, KT, 2):
                sp.wait_ge(out_ready, kt + 2)
                sp.dma_start(out[kt:kt + 2].rearrange("k p t -> p k t"), x[:, kt:kt + 2, :]).then_inc(out_sent, 16)
            sp.wait_ge(out_sent, 16 * KT // 2)

        @block.tensor
        def _(pe):
            mm = nc.tensor.matmul

            def product(p, g, o, pieces):
                count = p.out_count(g, o)
                dst = acc[o % 2]
                if not isinstance(count, int) or count > 2:
                    pe.wait_ge(evac_done, count - 2)
                for i, (m, t0, n, moving, k0) in enumerate(pieces):
                    whole, s = p.tiles_of(m), m % SLOTS
                    if t0 == 0:
                        pe.wait_ge(lo_done, p.weight_count(g, m))
                    for t in range(n):
                        end = i == len(pieces) - 1 and t == n - 1
                        mm(dst[:], hi[s][:, t0 + t, :], moving[:, k0 + t, :], start=i == 0 and t == 0, stop=False,
                           skip_group_check=True)
                        ins = mm(dst[:, T:], lo[s][:, t0 + t, :], moving[:, k0 + t, 0:T], start=False, stop=end,
                                 skip_group_check=True)
                    if t0 + n == whole:
                        ins.then_inc(slot_free[s], 1)
                    elif i == len(pieces) - 1:
                        ins.then_inc(part_done, 1)

            def opening_pair(p, ready):
                pe.wait_ge(lo_done, p.weight_count(0, 1))
                if p.first_out:
                    pe.wait_ge(evac_done, p.first_out)
                for t in range(KT):
                    pe.wait_ge(h_done, ready + t + 1)
                    for o in range(2):
                        mm(acc[o][:], hi[o][:, t, :], h[:, t, :], start=t == 0, stop=False, skip_group_check=True)
                        ins = mm(acc[o][:, T:], lo[o][:, t, :], h[:, t, 0:T], start=False, stop=t == KT - 1,
                                 skip_group_check=True)
                        if t == KT - 1:
                            ins.then_inc(slot_free[o], 1)

            def add_squares(stage):
                if stage:
                    pe.wait_ge(std_done, stage)
                for kt in range(KT):
                    pe.wait_ge(sq_done, KT * stage + kt + 1)
                    mm(p_norm[:, 0:T], ones[:], tile[kt % 2][:], start=kt == 0, stop=kt == KT - 1).then_inc(sq_used, 1)

            def add_features(stage):
                pe.wait_ge(sq_used, KT * (stage + 1))
                mm(p_norm[:, 0:T], ones[:], sq_sum[:], start=True, stop=True).then_inc(sums_done, 1)

            def s5_steps(name, g, m, tail=False):
                base = 4 * S5_FIRST[name]
                for i, tile in s5_due(name, g, m):
                    ut = g + tile // 4
                    pe.wait_ge(s5_c_in[i % 2], 32 * g + 16 * (tile // 2 + 1))
                    pe.wait_ge(scan_done, 4 * g + (tile + 1))
                    if i == 0 and not (isinstance(ut, int) and ut == 0):
                        pe.wait_ge(s5_y_done, ut)
                    for c in range(2):
                        ins = mm(p_y[:, 0:T], s5_c[i % 2][:, c, :], s5_x[i % 2][:, c, :], start=i == 0 and c == 0,
                                 stop=i == 3 and c == 1)
                    ins.then_inc(y_part, 1)
                if not tail and m in S5_Z:
                    i = S5_Z.index(m)
                    before = 4 * g + (base + i)
                    pe.wait_ge(s5_b_in[i % 2], 32 * g + 16 * (base // 2 + i // 2 + 1))
                    if not (isinstance(before, int) and before == 0):
                        pe.wait_ge(x_ready, before)
                    for c in range(2):
                        ins = mm(p_z[:, c * T:(c + 1) * T], s5_b[i % 2][:, c, :], u[:, g + S5_FIRST[name], :],
                                 start=True, stop=True)
                    ins.then_inc(z_done, 1)

            pe.wait_ge(ones_set, 2)
            pe.wait_ge(start_in, 16 * 8)
            add_squares(0)

            p = ph["u"]
            opening_pair(p, 0)
            for g in range(p.iters):
                for o in range(2 if g == 0 else 0, 4):
                    product(p, g, o, [(o, 0, 16, h, 0)])

            def ret_scores(g, i, n):
                pe.wait_ge(evac_done, ph["heads"].out_count(g, 6 * i - 3))
                for s in range(2):
                    for j in range(2):
                        ins = nc.tensor.transpose(p_turn[:, s * T + j * P:s * T + (j + 1) * P],
                                                  v_t[:, j, s * P:(s + 1) * P], ident[:])
                ins.then_inc(R["turned"], 1)
                pe.wait_ge(R["rope"], n)
                mm(p_score[:, 0:T], qk_rot[:, 1, 0:P], qk_rot[:, 0, :], start=True, stop=True)
                mm(p_score[:, T:T + P], qk_rot[:, 1, P:T], qk_rot[:, 0, P:T], start=True, stop=True).then_inc(R["scored"], 1)

            def ret_values(g, i, n):
                pe.wait_ge(R["v_n"], n)
                pe.wait_ge(R["masked"], n)
                for j in range(2):
                    mm(p_o[:, j * T:(j + 1) * T], v_n[:, 0, j * P:(j + 1) * P], scores[:, 0:T], start=True, stop=False)
                    ins = mm(p_o[:, j * T + P:(j + 1) * T], v_n[:, 1, j * P:(j + 1) * P], scores[:, T:T + P],
                             start=False, stop=True)
                ins.then_inc(R["summed"], 1)

            def ret_mean(g, i, n):
                pe.wait_ge(R["o"], n)
                mm(p_norm[:, 0:T], ones[:], o_t[:, 0, :], start=True, stop=False)
                mm(p_norm[:, 0:T], ones[:], o_t[:, 1, :], start=False, stop=True).then_inc(R["mean"], 1)

            def ret_var(g, i, n):
                pe.wait_ge(R["sq"], n)
                mm(p_norm[:, T:], ones[:], qk_sin[:, 0, :], start=True, stop=False)
                mm(p_norm[:, T:], ones[:], qk_sin[:, 1, :], start=False, stop=True).then_inc(R["var"], 1)

            steps = [ret_scores, ret_values, ret_mean, ret_var]
            p = ph["heads"]
            pe.wait_ge(s5_trig, 1)
            for g in bodies(pe, p, first=1):
                for m in range(12):
                    i, r = divmod(m, 6)
                    product(p, g, m, [(m, 0, 16, h, 0)])
                    if r < 4 and not (opening(g) and m < 6):
                        steps[r](g, i, 2 * g + i)
                    s5_steps("heads", g, m)
            for step in steps:
                step(p.iters, 0, HEADS)

            p = ph["ret"]
            for g in bodies(pe, p, first=1):
                for m in range(8):
                    if m % 2:
                        pe.wait_ge(R["done"], HEADS)
                    product(p, g, m, [(m, 0, 16, ret_flat if m % 2 else h, 0)])
                    s5_steps("ret", g, m)
            for m in S5_TAIL:
                s5_steps("ret", p.iters, m, tail=True)

            p = ph["glu"]
            for g in bodies(pe, p):
                for i in range(4):
                    product(p, g, 3 * i, [(2 * i, 0, 16, h, 0)])
                    pe.wait_ge(s5_done, HALF)
                    for c in range(2):
                        product(p, g, 3 * i + 1 + c, [(2 * i + 1, 8 * c, 8, y_ssm, 0)])

            def full_width(p, pieces, stage):
                for g in bodies(pe, p):
                    for o in range(4):
                        product(p, g, o, pieces(o))
                add_features(stage)

            def narrow(moving):
                return lambda o: [(o, 0, 16, moving, 0)]

            def wide(moving):
                return lambda o: [(3 * o, 0, 16, moving, 0), (3 * o + 1, 0, 16, moving, 16), (3 * o + 2, 0, 12, moving, 32)]

            pe.wait_ge(mm_split, KT)
            full_width(ph["out1"], narrow(merged), 1)
            add_squares(2)

            def hidden(p, ready=None):
                if ready is not None:
                    opening_pair(p, ready)
                for g in bodies(pe, p, first=ready is not None):
                    for m in range(2 if ready is not None and opening(g) else 0, 8):
                        product(p, g, m, [(m, 0, 16, h, 0)])

            hidden(ph["ffa"], KT)
            hidden(ph["ffb"])
            pe.wait_ge(f_split, FF)
            full_width(ph["down1"], wide(f1), 3)
            add_squares(4)

            def att_scores(g, i, n, par):
                pe.wait_ge(evac_done, ph["att"].out_count(g, 3 * i - 1))
                for s in range(2):
                    ins = nc.tensor.transpose(p_turn[:, s * P:(s + 1) * P], att_v[par][:, s * P:(s + 1) * P], ident[:])
                ins.then_inc(A["turned"], 1)
                for s in range(2):
                    ins = mm(p_score[:, s * T:(s + 1) * T], att_q[par][:, s * P:(s + 1) * P], att_k[par][:],
                             start=True, stop=True)
                ins.then_inc(A["scored"], 1)

            def att_turn(g, i, n, par):
                pe.wait_ge(A["p"], n)
                nc.tensor.transpose(p_z[:, 0:P], ex[:, 0, 0:P], ident[:])
                nc.tensor.transpose(p_z[:, P:T], ex[:, 1, 0:P], ident[:])
                nc.tensor.transpose(p_z[:, T:T + P], ex[:, 1, P:T], ident[:]).then_inc(A["p_turned"], 1)

            def att_values(g, i, n, par):
                pe.wait_ge(A["p_t"], n)
                pe.wait_ge(A["v_n"], n)
                mm(p_o[:, 0:T], av_n[:, 0, :], ex_t[:, 0:T], start=True, stop=False)
                mm(p_o[:, P:T], av_n[:, 1, :], ex_t[:, T:T + P], start=False, stop=True).then_inc(A["summed"], 1)

            def gate_down():
                pe.wait_ge(B0["lo"], 1)
                for k in range(KT):
                    mm(p_score[0:RANK, :], wa_hi[:, k, :], h[:, k, :], start=k == 0, stop=False, skip_group_check=True)
                    ins = mm(p_score[0:RANK, T:], wa_lo[:, k, :], h[:, k, 0:T], start=False, stop=k == KT - 1,
                             skip_group_check=True)
                ins.then_inc(B0["down"], 1)

            def gate_up():
                pe.wait_ge(B0["ad"], 1)
                for n in range(GLA_HEADS):
                    ins = mm((p_turn if n < 2 else p_o)[:, n % 2 * T:(n % 2 + 1) * T], gla_up[:, n * P:(n + 1) * P], gla_ad[:],
                             start=True, stop=True)
                ins.then_inc(B0["z"], 1)

            steps = [att_scores, att_turn, att_values]
            p = ph["att"]
            opening_pair(p, 2 * KT)
            for g in bodies(pe, p, first=1):
                for m in range(12):
                    i, r = divmod(m, 3)
                    if not (opening(g) and m < 2):
                        product(p, g, m, [(m, 0, 16, h, 0)])
                    if not (opening(g) and i == 0):
                        steps[r](g, i, 4 * g + i, (i + 1) % 2)
                    elif r == 0:
                        gate_down()
                    elif r == 1:
                        gate_up()
            for step in steps:
                step(p.iters, 0, HEADS, 1)

            def gla_scores(g, i, n, par):
                pe.wait_ge(evac_done, ph["gla"].out_count(g, 6 * i - 3))
                for s in range(2):
                    for j in range(2):
                        nc.tensor.transpose(p_turn[:, s * T + j * P:s * T + (j + 1) * P],
                                            gv_t[:, j, s * P:(s + 1) * P], ident[:])
                pe.wait_ge(B["qk"], n)
                for s in range(2):
                    ins = nc.tensor.transpose(p_z[:, s * P:(s + 1) * P], k_dec[:, s * P:(s + 1) * P], ident[:])
                ins.then_inc(B["turned"], 1)
                for s in range(2):
                    ins = mm(p_score[:, s * P:(s + 1) * P], k_in[:, s * P:(s + 1) * P], q_in[par][:, s * P:(s + 1) * P],
                             start=True, stop=True)
                ins.then_inc(B["scored"], 1)

            def gla_states(g, i, n, par):
                pe.wait_ge(B["v_n"], n)
                for c, dst in enumerate((p_y[:, 0:T], p_y[:, T:], p_z[:, T:])):
                    ins = mm(dst, k_dec_n[:, c, :], gv_n[:, c // 2, :], start=True, stop=True)
                ins.then_inc(B["kv"], 1)

            def gla_values(g, i, n, par):
                pe.wait_ge(B["intra"], n)
                pe.wait_ge(B["states"], n)
                for j in range(2):
                    for s in range(2):
                        mm(p_o[:, j * T + s * P:j * T + (s + 1) * P], gv_n[:, s, j * P:(j + 1) * P], intra[:, s, :],
                           start=True, stop=False)
                        for c in range(max(1, 2 * s), 2 * s + 2):
                            ins = mm(p_o[:, j * T + 64 * c:j * T + 64 * c + 64], state[c - 1][:, j * P:(j + 1) * P],
                                     q_in[par][:, 64 * c:64 * c + 64], start=False, stop=c == 2 * s + 1)
                ins.then_inc(B["summed"], 1)

            def gla_var(g, i, n, par):
                pe.wait_ge(B["o"], n)
                mm(p_norm[:, 0:T], ones[:], go_sq[:, 0, :], start=True, stop=False)
                mm(p_norm[:, 0:T], ones[:], go_sq[:, 1, :], start=False, stop=True).then_inc(B["var"], 1)

            steps = {0: gla_scores, 1: gla_states, 3: gla_values, 4: gla_var}
            p = ph["gla"]
            for g in bodies(pe, p, first=1):
                for m in range(12):
                    i, r = divmod(m, 6)
                    product(p, g, m, [(m, 0, 16, h, 0)])
                    if r in steps and not (opening(g) and i == 0):
                        steps[r](g, i, 2 * g + i, (i + 1) % 2)
            for step in steps.values():
                step(p.iters, 0, GLA_HEADS, 1)

            for name in ("conv", "mrg0"):
                p = ph[name]
                for g in bodies(pe, p):
                    for m in range(p.outs):
                        product(p, g, m, [(m, 0, 16, h, 0)])

            p = ph["mix"]
            pe.wait_ge(A["done"], HEADS)
            pe.wait_ge(B["done"], GLA_HEADS)
            pe.wait_ge(cv_split, HALF)
            for g in bodies(pe, p):
                for i in range(2):
                    for c in range(2):
                        product(p, g, 5 * i + c, [(4 * i + c, 0, 16, h, 0)])
                    product(p, g, 5 * i + 2, [(4 * i + 2, 0, 8, o_att, 0)])
                    product(p, g, 5 * i + 3, [(4 * i + 2, 8, 8, gla_flat, 0)])
                    product(p, g, 5 * i + 4, [(4 * i + 3, 0, 8, y_conv, 0)])

            pe.wait_ge(mx_split, KT)
            full_width(ph["out2"], narrow(mixed), 5)
            hidden(ph["ff2"], 3 * KT)
            pe.wait_ge(f_split, 2 * FF)
            full_width(ph["down2"], wide(f2), 6)

        @block.scalar
        def _(act):
            run = nc.scalar.activation
            own = Own(act, act_own)
            COPY = ACT.Copy

            def split_hi(p, g, m):
                n, s = p.tiles_of(m), m % SLOTS
                act.wait_ge(raw_in[s], p.uses(g, m) * 16)
                run(hi[s][:, 0:n, :], raw[s][:, 0:n, :], COPY).then_inc(hi_done, 1)

            def half_out(p, g, o, m, part=None):
                s = m % SLOTS
                count = p.out_count(g, o)
                if part is None:
                    act.wait_ge(slot_free[s], p.uses(g, m))
                else:
                    act.wait_ge(part_done, part)
                if not isinstance(count, int) or count > 2:
                    act.wait_ge(evac_done, count - 2)
                run(half[o % 2][:], acc[o % 2][:, T:], COPY).then_inc(half_done, 1)

            def ahead(p, g, m, end=False):
                if not (end and m + 2 >= len(p.tiles) or p.opens and opening(g) and m < 2):
                    split_hi(p, g, m + 2)

            def evacuated(p, g, o):
                act.wait_ge(evac_done, p.out_count(g, o))

            def ada_aside(name, g, i, tile):
                k = i % 2
                buffer, count = aside[name][k], ph[name].aside_count(g, i)
                act.wait_ge(aside_mul[k], pool_count(name, g, i))
                run(buffer[:], buffer[:], COPY, accum_out=ada_sum[:, 5:6]).then_inc(aside_free[k], 1)
                act.wait_ge(aside_free[k], count)
                run(mod[:, one(tile)], ada_sum[:, 5:6], ACT.Identity, bias=b_ada[:, one(tile)], scale=0.5).then_inc(mod_done, 1)

            def square_of(stage, src, kt, par):
                n = kt + (16 * stage)
                if not isinstance(n, int) or n >= 2:
                    act.wait_ge(sq_used, n - 1)
                run(tile[par][:], src, ACT.Square).then_inc(sq_done, 1)

            def std_of(stage):
                if stage in BY_PE:
                    act.wait_ge(sq_used, KT * (stage + 1))
                else:
                    act.wait_ge(sums_done, len([n for n in range(stage + 1) if n not in BY_PE]))
                run(rstd[:], p_norm[:, 0:T], ACT.Sqrt, bias=eps[:, 0:1], scale=1.0 / D).then_inc(std_done, 1)

            def residual_squares(stage, updates):
                with act.Fori(0, KT // 8) as q:
                    for b in range(8):
                        act.wait_ge(y_done, 8 * q + (16 * updates + b + 1))
                        square_of(stage, x[:, 8 * q + b, :], 8 * q + b, b % 2)

            def split_h(stage, shift=None):
                with act.Fori(0, KT // 8) as q:
                    for b in range(8):
                        k = 8 * q + b
                        act.wait_ge(n_done, k + (16 * stage + 1))
                        if shift is None:
                            ins = run(h[:, k, 0:T], normed[:, k, T:], COPY)
                        else:
                            ins = run(h[:, k, 0:T], normed[:, k, T:], ACT.Identity, bias=mod[:, one(8 * q + (shift + b))])
                        ins.then_inc(n_hi, 1)

            def start():
                for dst, name in ((s5_a, "s5_a"), (gains, "gains"), (b_ada, "b_ada_c"), (ident, "identity"), (rope, "rope"),
                                  (lag, "lag"), (log_g, "log_g"), (s5_d, "s5_d")):
                    act.dma_start(dst[:], dram[name]).then_inc(start_in, 16)
                act.dma_start(s5_b[0][:], dram["s5_b"][0]).then_inc(s5_b_in[0], 16)
                act.wait_ge(c_in, 16)
                run(c_tanh_half[:], c_act[:], ACT.Tanh, scale=0.5).then_inc(c_tanh, 1)
                act.dma_start(x[:], dram["x_t"]).then_inc(x_in, 16)
                act.wait_ge(start_in, 16 * 8)
                run(s5_t[:, 0, :], s5_a[:, 2, :], ACT.Exp).then_inc(s5_trig, 1)
                act.wait_ge(s5_params, 1)
                run(s5_t[:, 1, :], s5_t[:, 1, :], ACT.Exp)
                own.step(run(s5_t[:, 4, :], s5_t[:, 3, :], ACT.Sin, scale=0.5))
                run(s5_t[:, 3, :], s5_t[:, 3, :], ACT.Sin).then_inc(s5_trig, 1)
                act.wait_ge(x_in, 16)
                for kt in range(KT):
                    square_of(0, x[:, kt, :], kt, kt % 2)
                act.wait_ge(ones_set, 2)
                std_of(0)
                split_hi(ph["u"], 0, 0)
                split_hi(ph["u"], 0, 1)
                split_hi(ph["u"], 0, 2)
                split_h(0, 0)
                split_hi(ph["u"], 0, 3)

            def s5_steps(name, g, m, early, tail=False, end=False):
                first = S5_FIRST[name]
                if early:
                    n = len(ph[name].tiles)
                    if not tail and (m + 1) % n in S5_Z and not (m + 1 == n and end):
                        i = S5_Z.index((m + 1) % n)
                        s = 4 * g + (4 * (first + (m + 1) // n) + i)
                        if not isinstance(s, int) or s >= 2:
                            act.wait_ge(z_done, s - 1)
                        act.dma_start(s5_b[i % 2][:], dram["s5_b"][s]).then_inc(s5_b_in[i % 2], 16)
                    for i, tile in s5_due(name, g, m, lead=1):
                        s = 4 * g + tile
                        if not isinstance(s, int) or s >= 2:
                            act.wait_ge(y_part, s - 1)
                        act.dma_start(s5_c[i % 2][:], dram["s5_c"][s]).then_inc(s5_c_in[i % 2], 16)
                    return
                if not tail and m in S5_Z:
                    i = S5_Z.index(m)
                    s = 4 * g + (4 * first + i)
                    now = s5_now[i % 2]
                    if not isinstance(s, int) or s >= 2:
                        act.wait_ge(y_part, s - 1)
                    own.step(run(now[:], s5_p[:, s, :], COPY))
                    act.wait_ge(z_done, s + 1)
                    run(s5_x[i % 2][:, 0, :], p_z[:, T:], COPY, scale=now[:, 34:35])
                    run(s5_x[i % 2][:, 1, :], p_z[:, 0:T], COPY, scale=now[:, 34:35]).then_inc(x_half, 1)
                if (S5_TILES // HALF - 1) in [i for i, _ in s5_due(name, g, m)]:
                    ut = g + s5_due(name, g, m)[0][1] // 4
                    n = g + (s5_due(name, g, m)[0][1] // 4 + 1)
                    act.wait_ge(s5_y_done, n)
                    run(s5_g[:], s5_y[:], ACT.Square).then_inc(s5_sq, 1)
                    act.wait_ge(s5_in, n)
                    run(s5_g[:], s5_g[:], ACT.Tanh, scale=GELU_IN).then_inc(s5_tanh, 1)
                    act.wait_ge(s5_m, n)
                    run(y_ssm[:, ut, 0:T], s5_y[:], COPY, scale=0.5).then_inc(s5_hi, 1)

            def ret_step(r, g, i, n):
                if r == 0:
                    evacuated(ph["heads"], g, 6 * i - 1)
                    run(g_act[:], g_t[:], ACT.Tanh, scale=0.5).then_inc(R["tanh"], 1)
                    act.wait_ge(R["turned"], n)
                    run(v_n[:].rearrange("p s v -> p (s v)"), p_turn[:], COPY).then_inc(R["v_n"], 1)
                elif r == 1:
                    act.wait_ge(R["summed"], n)
                    run(o_t[:].rearrange("p j t -> p (j t)"), p_o[:], COPY).then_inc(R["o"], 1)
                elif r == 2:
                    act.wait_ge(R["dev"], n)
                    run(qk_sin[:], o_t[:], ACT.Square).then_inc(R["sq"], 1)
                elif r == 4:
                    act.wait_ge(R["var"], n)
                    run(std[:], p_norm[:, T:], ACT.Sqrt, bias=eps[:, 1:2], scale=1.0 / V_DIM).then_inc(R["std"], 1)
                elif r == 5:
                    act.wait_ge(R["out"], n)
                    run(ret[:, 2 * g + i - 1, :, 0:T], o_t[:], COPY, scale=0.5).then_inc(R["hi"], 1)

            start()
            p = ph["u"]
            for g in range(p.iters):
                for m in range(4):
                    ahead(p, g, m)
                    half_out(p, g, m, m)
            act.wait_ge(s5_params, 2)

            p = ph["heads"]
            for g in bodies(act, p, first=1):
                own.enter(4, g, first=1)
                for m in range(12):
                    i, r = divmod(m, 6)
                    ahead(p, g, m)
                    s5_steps("heads", g, m, early=True)
                    half_out(p, g, m, m)
                    if not (opening(g) and i == 0):
                        ret_step(r, g, i, 2 * g + i)
                    if r == 3:
                        n = 2 * g + i
                        if not (opening(g) and i == 0):
                            act.wait_ge(R["masked"], n)
                        run(scores[:, 0:T], lag[:], ACT.Exp, scale=log_g[:, one(n)])
                        run(scores[:, T:], lag[:, 0:P], ACT.Exp, scale=log_g[:, one(n)]).then_inc(R["decay"], 1)
                    s5_steps("heads", g, m, early=False)
                own.leave(1 if isinstance(g, int) else p.iters - 1)
            for r in range(6):
                ret_step(r, p.iters, 0, HEADS)

            p = ph["ret"]
            for g in bodies(act, p, first=1, last=1):
                own.enter(4, g, first=1)
                for m in range(8):
                    ahead(p, g, m)
                    s5_steps("ret", g, m, early=True, end=isinstance(g, int) and g > 0)
                    if m % 2:
                        evacuated(p, g, m - 1)
                        run(gate[:], gate[:], ACT.Tanh, scale=0.5).then_inc(gr_tanh, 1)
                    half_out(p, g, m, m)
                    s5_steps("ret", g, m, early=False)
                own.leave(1 if isinstance(g, int) else p.iters - 2)
            for m in S5_TAIL:
                s5_steps("ret", p.iters, m - 1, early=True, tail=True)
                s5_steps("ret", p.iters, m, early=False, tail=True)

            p = ph["glu"]
            for g in bodies(act, p):
                for i in range(4):
                    if i == 0:
                        ahead(p, g, 0)
                    half_out(p, g, 3 * i, 2 * i)
                    ahead(p, g, 2 * i + 1)
                    evacuated(p, g, 3 * i)
                    run(gate[:], gate[:], ACT.Tanh, scale=0.5).then_inc(gs_tanh, 1)
                    ada_aside("glu", g, i, 4 * g + (3 * KT + 8 + i))
                    half_out(p, g, 3 * i + 1, 2 * i + 1, part=4 * g + (i + 1))
                    half_out(p, g, 3 * i + 2, 2 * i + 1)
                    evacuated(p, g, 3 * i + 2)
                    run(val_b[:], val_b[:], ACT.Tanh, scale=0.5).then_inc(gb_tanh, 1)
                    if i < 3:
                        ahead(p, g, 2 * i + 2)
                    act.wait_ge(mm_done, 4 * g + (i + 1))
                    run(merged[:, 4 * g + i, 0:T], val_a[:], COPY, scale=0.5).then_inc(mm_hi, 1)

            def down(p, stage, y, blocks, updates=None):
                for g in bodies(act, p, last=updates == 3):
                    end = updates == 3 and isinstance(g, int)
                    for m in range(4 * blocks):
                        ahead(p, g, m, end)
                        if m % blocks == blocks - 1:
                            o = m // blocks
                            half_out(p, g, o, m)
                            if p.asides and o == 3:
                                ada_aside("out1", g, 1, 2 * g + (4 * KT + 9))
                            if updates is None:
                                evacuated(p, g, o)
                            else:
                                act.wait_ge(y_done, 4 * g + (16 * updates + o + 1))
                            square_of(stage, y[:, 4 * g + o, :], 4 * g + o, o % 2)

            def ffn(p, pair0, dst, first, a, t):
                for g in bodies(act, p, first=p.opens):
                    for i in range(4):
                        ahead(p, g, 2 * i)
                        half_out(p, g, 2 * i, 2 * i)
                        ahead(p, g, 2 * i + 1)
                        if p.asides and i % 2:
                            ada_aside("ffa", g, i, 4 * g + (5 * KT + i))
                        evacuated(p, g, 2 * i)
                        run(t[i % 2][:], a[i % 2][:], ACT.Tanh, scale=0.5).then_inc(f_tanh, 1)
                        half_out(p, g, 2 * i + 1, 2 * i + 1)
                        act.wait_ge(f_done, 4 * g + (pair0 + i + 1))
                        run(dst[:, 4 * g + (first + i), 0:T], a[i % 2][:], COPY, scale=0.5).then_inc(f_hi, 1)

            down(ph["out1"], 1, y1, 1)
            split_hi(ph["ffa"], 0, 2)
            std_of(1)
            split_hi(ph["ffa"], 0, 3)
            residual_squares(2, 0)
            std_of(2)
            split_h(1, 3 * KT)
            ffn(ph["ffa"], 0, f1, 0, f1_a, f1_t)
            ffn(ph["ffb"], 16, f1, 16, f1_a, f1_t)
            down(ph["down1"], 3, y2, 3)

            for dst, name in ((wa_raw, "gla_down"), (ago, "ago"), (slopes, "slopes"), (causal, "chunk_causal"),
                              (carry, "chunk_carry"), (gla_up, "gla_up"), (gla_b, "gla_b"), (gla_norm, "gla_norm"),
                              (conv_w, "conv_w")):
                act.dma_start(dst[:], dram[name]).then_inc(late_in, 16)
            split_hi(ph["att"], 0, 2)
            std_of(3)
            split_hi(ph["att"], 0, 3)
            residual_squares(4, 1)
            std_of(4)
            split_h(2)
            act.wait_ge(late_in, 16 * 9)
            run(wa_hi[:], wa_raw[:], COPY).then_inc(B0["hi"], 1)

            def gate_half():
                act.wait_ge(B0["down"], 1)
                run(gla_ad[:], p_score[0:RANK, T:], COPY).then_inc(B0["half"], 1)

            def gate_decays():
                act.wait_ge(B0["z"], 1)
                for n in range(GLA_HEADS):
                    ins = run(a_in[:, n, :], (p_turn if n < 2 else p_o)[:, n % 2 * T:(n % 2 + 1) * T], ACT.Identity,
                              bias=gla_b[:, n:n + 1])
                ins.then_inc(B0["zb"], 1)
                act.wait_ge(B0["abs"], 1)
                own.step(run(a_out[:], a_out[:], ACT.Exp, scale=-1.0))
                run(a_out[:], a_out[:], ACT.Ln, bias=1.0).then_inc(B0["ln"], 1)
                act.wait_ge(B0["cum"], 1)
                run(a_in[:], log_a[:], ACT.Exp, scale=1.0 / GLA_TAU)
                run(a_out[:], log_a[:], ACT.Exp, scale=-1.0 / GLA_TAU)
                for n in range(GLA_HEADS):
                    for c in range(GLA_CHUNKS):
                        at = slice(64 * c, 64 * c + 64)
                        ins = run(a_end[:, n, at], log_a[:, n, at], ACT.Exp, bias=a_last[:, n, c:c + 1], scale=-1.0 / GLA_TAU)
                ins.then_inc(B0["decays"], 1)

            def att_step(r, g, i, n):
                if r == 0:
                    act.wait_ge(A["turned"], n)
                    run(av_n[:].rearrange("p s v -> p (s v)"), p_turn[:, 0:T], COPY).then_inc(A["v_n"], 1)
                    act.wait_ge(A["max"], n)
                    for s in range(2):
                        ins = run(ex[:, s, :], pre[:, s, :], ACT.Exp, bias=sm[:, 1, s:s + 1], scale=QK_SCALE,
                                  accum_out=sm[:, 2, s:s + 1])
                    ins.then_inc(A["exp"], 1)
                elif r == 1:
                    act.wait_ge(A["p_turned"], n)
                    run(ex_t[:], p_z[:, 0:T + P], COPY).then_inc(A["p_t"], 1)
                else:
                    act.wait_ge(A["summed"], n)
                    run(o_att[:, 4 * g + i - 1, 0:T], p_o[:, 0:T], COPY).then_inc(A["hi"], 1)

            p = ph["att"]
            for g in bodies(act, p, first=1):
                for m in range(12):
                    i, r = divmod(m, 3)
                    ahead(p, g, m)
                    half_out(p, g, m, m)
                    if not (opening(g) and i == 0):
                        att_step(r, g, i, 4 * g + i)
                    elif r == 0:
                        gate_half()
                    elif r == 1:
                        gate_decays()
            for r in range(3):
                att_step(r, p.iters, 0, HEADS)

            def gla_step(r, g, i, n):
                if r == 0:
                    evacuated(ph["gla"], g, 6 * i - 1)
                    run(gr_act[:], gr_t[:], ACT.Tanh, scale=0.5).then_inc(B["tanh"], 1)
                    act.wait_ge(B["turned"], n)
                    run(gv_n[:].rearrange("p s v -> p (s v)"), p_turn[:], COPY)
                    run(k_dec_n[0:64, 0, :], p_z[0:64, 0:P], COPY)
                    run(k_dec_n[64:P, 1, :], p_z[64:P, 0:P], COPY)
                    run(k_dec_n[0:64, 2, :], p_z[0:64, P:T], COPY).then_inc(B["v_n"], 1)
                elif r == 1:
                    act.wait_ge(B["kv"], n)
                    run(state[0][:], p_y[:, 0:T], COPY).then_inc(B["s1"], 1)
                elif r == 3:
                    act.wait_ge(B["summed"], n)
                    run(go[:].rearrange("p j t -> p (j t)"), p_o[:], COPY)
                    run(go_sq[:].rearrange("p j t -> p (j t)"), p_o[:], ACT.Square).then_inc(B["o"], 1)
                elif r == 4:
                    act.wait_ge(B["var"], n)
                    run(go_std[:], p_norm[:, 0:T], ACT.Sqrt, bias=eps[:, 0:1], scale=1.0 / V_DIM).then_inc(B["std"], 1)
                elif r == 5:
                    act.wait_ge(B["out"], n)
                    for j in range(2):
                        ins = run(o_gla[:, 2 * g + i - 1, j, 0:T], go[:, j, :], COPY, scale=gla_norm[:, j:j + 1])
                    ins.then_inc(B["hi"], 1)

            p = ph["gla"]
            for g in bodies(act, p, first=1):
                for m in range(12):
                    i, r = divmod(m, 6)
                    ahead(p, g, m)
                    half_out(p, g, m, m)
                    if not (opening(g) and i == 0):
                        gla_step(r, g, i, 2 * g + i)
            for r in range(6):
                gla_step(r, p.iters, 0, GLA_HEADS)

            p = ph["conv"]
            for g in bodies(act, p):
                for m in range(12):
                    ahead(p, g, m)
                    half_out(p, g, m, m)
                    if m % 3 == 2:
                        act.wait_ge(cv_done, 4 * g + (m // 3 + 1))
                        run(y_conv[:, 4 * g + m // 3, 0:T], cy[:], COPY).then_inc(cv_hi, 1)

            p = ph["mrg0"]
            for g in bodies(act, p):
                for m in range(4):
                    ahead(p, g, m)
                    half_out(p, g, m, m)
                    evacuated(p, g, m)
                    run(t0[:, 4 * g + m, :], mg[m % 2][:], ACT.Tanh, scale=0.5).then_inc(t0_done, 1)

            p = ph["mix"]
            for g in bodies(act, p):
                for i in range(2):
                    ahead(p, g, 4 * i)
                    half_out(p, g, 5 * i, 4 * i)
                    ahead(p, g, 4 * i + 1)
                    evacuated(p, g, 5 * i)
                    run(mg[0][:], mg[0][:], ACT.Tanh, scale=0.5)
                    half_out(p, g, 5 * i + 1, 4 * i + 1)
                    ahead(p, g, 4 * i + 2)
                    evacuated(p, g, 5 * i + 1)
                    run(mg[1][:], mg[1][:], ACT.Tanh, scale=0.5).then_inc(mt_done, 1)
                    half_out(p, g, 5 * i + 2, 4 * i + 2, part=2 * g + (KT + i + 1))
                    half_out(p, g, 5 * i + 3, 4 * i + 2)
                    ahead(p, g, 4 * i + 3)
                    half_out(p, g, 5 * i + 4, 4 * i + 3)
                    act.wait_ge(mx_done, 2 * g + (i + 1))
                    run(mixed[:, 2 * g + i, 0:T], br[0][:], COPY, scale=0.5).then_inc(mx_hi, 1)

            down(ph["out2"], 5, x, 1, updates=2)
            split_hi(ph["ff2"], 0, 2)
            std_of(5)
            split_h(3)
            split_hi(ph["ff2"], 0, 3)
            ffn(ph["ff2"], FF, f2, 0, f2_a, f2_t)
            down(ph["down2"], 6, x, 3, updates=3)
            std_of(6)

        @block.vector
        def _(dve):
            v = nc.vector
            own = Own(dve, dve_own)
            tt, stt = v.tensor_tensor, v.scalar_tensor_tensor
            MUL, ADD, SUB = ALU.mult, ALU.add, ALU.subtract

            def split_lo(p, g, m):
                n, s = p.tiles_of(m), m % SLOTS
                dve.wait_ge(hi_done, p.weight_count(g, m))
                tt(lo[s][:, 0:n, :], raw[s][:, 0:n, :], hi[s][:, 0:n, :], SUB).then_inc(lo_done, 1)

            def ahead(p, g, m, end=False):
                if not (end and m + 2 >= len(p.tiles) or p.opens and opening(g) and m < 2):
                    split_lo(p, g, m + 2)

            def evac(p, g, o, dst, own_use=False):
                count = p.out_count(g, o)
                dve.wait_ge(half_done, count)
                tt(dst, acc[o % 2][:, 0:T], half[o % 2][:], ADD).then_inc(evac_done, 1)
                if own_use:
                    dve.wait_ge(evac_done, count)

            def ada(weights, landed, done, count, i, tile):
                dve.wait_ge(landed, 16 * count)
                v.tensor_tensor_reduce(weights, weights, c_act[:], 1.0, 0.0, MUL, ADD, ada_sum[:, i:i + 1]).then_inc(done, 1)
                dve.wait_ge(done, count)
                own.step(stt(mod[:, one(tile)], ada_sum[:, i:i + 1], 0.5, b_ada[:, one(tile)], MUL, ADD))

            def ada_aside(name, g, i, tile):
                k = i % ph[name].beside
                ada(aside[name][k][:], aside_in[k], aside_free[k], ph[name].aside_count(g, i), i, tile)

            def one_plus(i, n, t0):
                own.step(stt(gain[:, i, :], mod[:, t0:t0 + KT], 1.0, gains[:, n, :], ADD, MUL))

            def gated(i, n, t0):
                own.step(tt(gain[:, i, :], mod[:, t0:t0 + KT], gains[:, n, :], MUL))

            def inverse_std(stds):
                dve.wait_ge(std_done, stds)
                own.step(v.reciprocal(rstd[:], rstd[:]))

            def norm(stage, stds, by, shift=None):
                inverse_std(stds)
                def scaled(k):
                    stt(normed[:, k, T:], x[:, k, :], by(k), rstd[:], MUL, MUL).then_inc(n_done, 1)

                def split(k, shift_at):
                    dve.wait_ge(n_hi, k + (16 * stage + 1))
                    if shift is None:
                        ins = tt(h[:, k, T:], normed[:, k, T:], h[:, k, 0:T], SUB)
                    else:
                        ins = stt(h[:, k, T:], normed[:, k, T:], mod[:, one(shift_at)], h[:, k, 0:T], ADD, SUB)
                    ins.then_inc(h_done, 1)

                LEAD, STEP = 2, 7
                for k in range(LEAD):
                    scaled(k)
                with dve.Fori(0, (KT - LEAD) // STEP) as q:
                    for b in range(STEP):
                        scaled(STEP * q + (b + LEAD))
                        split(STEP * q + b, STEP * q + ((shift or 0) + b))
                for k in range(KT - LEAD, KT):
                    split(k, (shift or 0) + k)

            def residual(y, i, stds):
                inverse_std(stds)
                with dve.Fori(0, KT // 4) as q:
                    own.enter(4, q)
                    marks = []
                    for b in range(4):
                        k = 4 * q + b
                        marks.append(own.mark(stt(y[:, k, :], y[:, k, :], gain[:, i, one(k)], rstd[:], MUL, MUL)))
                    for b in range(4):
                        k = 4 * q + b
                        dve.wait_ge(dve_own, marks[b])
                        tt(x[:, k, :], x[:, k, :], y[:, k, :], ADD).then_inc(y_done, 1)
                    own.leave(KT // 4)

            def s5_angles():
                def half_op(dst, src, s1, op0, s2=None, op1=None):
                    own.step(v.tensor_scalar(dst, src, s1, s2, op0) if op1 is None else
                             v.tensor_scalar(dst, src, s1, s2, op0, op1))

                dve.wait_ge(s5_trig, 1)
                t = [s5_t[:, n, :] for n in range(12)]
                tt(t[1], s5_a[:, 0, :], t[0], MUL)
                own.step(tt(t[2], s5_a[:, 1, :], t[0], MUL))
                half_op(t[5], t[2], 1.0 / TURN, MUL)
                half_op(t[5], t[5], ROUND, ADD)
                half_op(t[5], t[5], -ROUND, ADD)
                own.step(stt(t[3], t[5], -TURN_HI, t[2], MUL, ADD))
                own.step(stt(t[3], t[5], -TURN_LO, t[3], MUL, ADD))
                v.tensor_scalar(t[3], t[3], PI_IN, -PI_IN, ALU.min, ALU.max).then_inc(s5_params, 1)

            def s5_powers():
                t = [s5_t[:, n, :] for n in range(12)]
                a_re, a_im = s5_a[:, 0, :], s5_a[:, 1, :]
                dve.wait_ge(s5_trig, 2)
                own.step(tt(t[5], t[4], t[4], MUL))
                own.step(v.tensor_scalar(t[5], t[5], -2.0, 1.0, MUL, ADD))
                power = [[s5_p[:, :, 4 * k + c] for c in range(4)] for k in range(LEVELS)]
                re, im, _, _ = power[0]
                tt(re, t[1], t[5], MUL)
                tt(im, t[1], t[3], MUL)
                tt(t[6], a_re, a_re, MUL)
                own.step(tt(t[7], a_im, a_im, MUL))
                own.step(tt(t[6], t[6], t[7], ADD))
                own.step(v.reciprocal(t[6], t[6]))
                own.step(v.tensor_scalar(t[7], re, -1.0, None, ADD))
                tt(t[8], t[7], a_re, MUL)
                tt(t[9], im, a_im, MUL)
                tt(t[10], im, a_re, MUL)
                own.step(tt(t[11], t[7], a_im, MUL))
                tt(t[8], t[8], t[9], ADD)
                own.step(tt(t[10], t[10], t[11], SUB))
                tt(s5_p[:, :, 32], t[8], t[6], MUL)
                own.step(stt(s5_p[:, :, 33], t[8], -1.0, t[6], MUL, MUL))
                own.step(stt(s5_p[:, :, 34], t[10], -1.0, t[6], MUL, MUL))
                for k in range(LEVELS):
                    re, im, neg, again = power[k]
                    v.tensor_scalar(neg, im, -1.0, None, MUL)
                    ins = v.tensor_copy(again, re)
                    if k + 1 < LEVELS:
                        tt(t[5], re, re, MUL)
                        tt(t[6], im, im, MUL)
                        own.step(stt(power[k + 1][1], re, 2.0, im, MUL, MUL))
                        own.step(tt(power[k + 1][0], t[5], t[6], SUB))
                ins.then_inc(s5_params, 1)

            v.memset(ones[:], 1.0).then_inc(ones_set, 1)
            v.memset(eps[:, 0:1], NORM_EPS)
            v.memset(eps[:, 1:2], GN_EPS).then_inc(ones_set, 1)
            dve.wait_ge(c_tanh, 1)
            own.step(stt(c_act[:], c_tanh_half[:], 1.0, c_act[:], ADD, MUL))
            s5_angles()
            p = ph["ada"]
            for g in bodies(dve, p, first=1):
                own.enter(4, g, first=1)
                for j in range(4):
                    ada(raw[j][:].rearrange("p k c -> p (k c)"), raw_in[j], slot_free[j], p.uses(g, j), j, 4 * g + j)
                own.leave(1 if isinstance(g, int) else p.iters - 1)
                if isinstance(g, int):
                    s5_powers()
            one_plus(0, 0, KT)
            split_lo(ph["u"], 0, 0)
            split_lo(ph["u"], 0, 1)
            norm(0, 1, lambda k: gain[:, 0, one(k)], 0)
            split_lo(ph["u"], 0, 2)
            split_lo(ph["u"], 0, 3)

            p = ph["u"]
            for g in range(p.iters):
                for o in range(4):
                    ahead(p, g, o)
                    if o >= 2:
                        ada_aside("u", g, o - 2, 2 * g + (2 * KT + o - 2))
                    evac(p, g, o, u[:, 4 * g + o, :])

            def carry_on(xs, now, to, frm):
                re, neg_im = xs[:, 0, :], xs[:, 1, :]
                stt(re[:, to], re[:, frm], now[:, 0:1], re[:, to], MUL, ADD)
                own.step(stt(neg_im[:, to], neg_im[:, frm], now[:, 0:1], neg_im[:, to], MUL, ADD))
                stt(re[:, to], neg_im[:, frm], now[:, 1:2], re[:, to], MUL, ADD)
                return stt(neg_im[:, to], re[:, frm], now[:, 2:3], neg_im[:, to], MUL, ADD)

            def s5_last(name, g, m):
                for i, tile in s5_due(name, g, m, lead=1):
                    dve.wait_ge(scan_core, 4 * g + (tile + 1))
                    carry_on(s5_x[i % 2], s5_now[i % 2], slice(2, T, 2), slice(1, T - 1, 2)).then_inc(scan_done, 1)

            def s5_steps(name, g, m, tail=False):
                first = S5_FIRST[name]
                if not tail and m in S5_Z:
                    i = S5_Z.index(m)
                    s = 4 * g + (4 * first + i)
                    dve.wait_ge(x_half, s + 1)
                    xs, now = s5_x[i % 2], s5_now[i % 2]
                    stt(xs[:, 0, :], p_z[:, 0:T], now[:, 32:33], xs[:, 0, :], MUL, ADD)
                    own.step(stt(xs[:, 1, :], p_z[:, T:], now[:, 33:34], xs[:, 1, :], MUL, ADD))
                    carry_on(xs, now, slice(1, T, 2), slice(0, T, 2)).then_inc(x_ready, 1)
                if (S5_TILES // HALF - 1) in [i for i, _ in s5_due(name, g, m)]:
                    ahead_by = s5_due(name, g, m)[0][1] // 4
                    ut = g + ahead_by
                    dve.wait_ge(y_part, 4 * g + 4 * (ahead_by + 1))
                    stt(s5_y[:], u[:, ut, :], s5_d[:, one(ut)], p_y[:, 0:T], MUL, ADD).then_inc(s5_y_done, 1)
                    dve.wait_ge(s5_sq, ut + 1)
                    own.step(v.tensor_scalar(s5_g[:], s5_g[:], GELU_CUBE, 1.0, MUL, ADD))
                    tt(s5_g[:], s5_g[:], s5_y[:], MUL).then_inc(s5_in, 1)
                    dve.wait_ge(s5_tanh, ut + 1)
                    stt(s5_y[:], s5_g[:], 1.0, s5_y[:], ADD, MUL).then_inc(s5_m, 1)
                    dve.wait_ge(s5_hi, ut + 1)
                    stt(y_ssm[:, ut, T:], s5_y[:], 0.5, y_ssm[:, ut, 0:T], MUL, SUB).then_inc(s5_done, 1)

            def pair(m):
                return m.unsqueeze(1).to_broadcast([P, 2, T])

            def ret_before(r, g, i, n):
                if r == 2:
                    dve.wait_ge(R["mean"], n)
                    stt(o_t[:], pair(p_norm[:, 0:T]), -1.0 / V_DIM, o_t[:], MUL, ADD).then_inc(R["dev"], 1)
                elif r == 5:
                    dve.wait_ge(R["std"], n)
                    own.step(v.reciprocal(std[:], std[:]))
                    own.step(tt(o_t[:], o_t[:], pair(std[:]), MUL))
                    tt(o_t[:], o_t[:], g_act[:], MUL).then_inc(R["out"], 1)

            def ret_after(r, g, i, n):
                if r == 0:
                    dve.wait_ge(R["scored"], n)
                    dve.wait_ge(R["decay"], n)
                    stt(scores[:], p_score[:, 0:384], QK_SCALE, scores[:], MUL, MUL).then_inc(R["masked"], 1)
                    dve.wait_ge(R["tanh"], n)
                    stt(g_act[:], g_act[:], 1.0, g_t[:], ADD, MUL)
                elif r == 5:
                    dve.wait_ge(R["hi"], n)
                    done = ret[:, 2 * g + i - 1, :, :]
                    stt(done[:, :, T:], o_t[:], 0.5, done[:, :, 0:T], MUL, SUB).then_inc(R["done"], 1)

            def rotate():
                tt(qk_rot[:], qk[:], pair(rope[:, 0, :]), MUL)
                for half_at, other in ((slice(0, 64), slice(64, P)), (slice(64, P), slice(0, 64))):
                    ins = tt(qk_sin[half_at], qk[other], rope[other, 1, :].unsqueeze(1).to_broadcast([64, 2, T]), MUL)
                own.step(ins)
                tt(qk_rot[:], qk_rot[:], qk_sin[:], ADD).then_inc(R["rope"], 1)

            ADA_AT = [1, 3, 6, 8, 10]
            p = ph["heads"]
            for g in bodies(dve, p, first=1):
                prev = [not opening(g), True]
                own.enter(2 + len(ADA_AT) + 4 * 3 + 1 + 2 * sum(prev), g, first=1)
                for m in range(12):
                    i, r = divmod(m, 6)
                    n = 2 * g + i
                    s5_last("heads", g, m)
                    if m in ADA_AT:
                        a = ADA_AT.index(m)
                        ada_aside("heads", g, a, 5 * g + (2 * KT + 4 + a))
                    ahead(p, g, m)
                    if prev[i]:
                        ret_before(r, g, i, n)
                    dst = (qk[:, 0, :], qk[:, 1, :], v_t[:, 0, :], v_t[:, 1, :], g_t[:, 0, :], g_t[:, 1, :])[r]
                    if r == 2 and prev[i]:
                        dve.wait_ge(R["turned"], n)
                    evac(p, g, m, dst, own_use=r == 1)
                    if r == 1:
                        rotate()
                    if prev[i]:
                        ret_after(r, g, i, n)
                    s5_steps("heads", g, m)
                own.leave(1 if isinstance(g, int) else p.iters - 1)
            for r in range(6):
                ret_before(r, p.iters, 0, HEADS)
                ret_after(r, p.iters, 0, HEADS)
            gated(1, 1, 2 * KT)

            p = ph["ret"]
            for g in bodies(dve, p, first=1):
                own.enter(4 * 2 + (3 if opening(g) else 4 + 1), g, first=1)
                for m in range(8):
                    d = 4 * g + m // 2
                    s5_last("ret", g, m)
                    ahead(p, g, m)
                    if m % 2:
                        evac(p, g, m, val_a[:], own_use=True)
                        dve.wait_ge(gr_tanh, d + 1)
                        stt(m_ret[:, d, :], gate[:], 1.0, val_a[:], ADD, MUL).then_inc(m_done, 1)
                        dve.wait_ge(m_done, d + 1)
                    else:
                        evac(p, g, m, gate[:])
                    s5_steps("ret", g, m)
                own.leave(1 if isinstance(g, int) else p.iters - 1)
            for m in S5_TAIL:
                s5_last("ret", p.iters, m - 1)
                s5_steps("ret", p.iters, m, tail=True)

            p = ph["glu"]
            for g in bodies(dve, p):
                own.enter(4 * 2, g)
                for i in range(4):
                    d = 4 * g + i
                    if i == 0:
                        ahead(p, g, 0)
                    evac(p, g, 3 * i, gate[:])
                    ahead(p, g, 2 * i + 1)
                    evac(p, g, 3 * i + 1, val_a[:])
                    evac(p, g, 3 * i + 2, val_b[:], own_use=True)
                    dve.wait_ge(gb_tanh, d + 1)
                    own.step(stt(val_b[:], val_b[:], 1.0, val_a[:], ADD, MUL))
                    own.step(stt(gate[:], gate[:], 1.0, val_b[:], ADD, MUL))
                    stt(val_a[:], gate[:], 0.5, m_ret[:, d, :], MUL, ADD).then_inc(mm_done, 1)
                    if i < 3:
                        ahead(p, g, 2 * i + 2)
                    dve.wait_ge(mm_hi, d + 1)
                    stt(merged[:, d, T:], val_a[:], 0.5, merged[:, d, 0:T], MUL, SUB).then_inc(mm_split, 1)
                own.leave(p.iters)

            p = ph["out1"]
            for g in bodies(dve, p):
                own.enter(1, g)
                for o in range(4):
                    ahead(p, g, o)
                    evac(p, g, o, y1[:, 4 * g + o, :])
                    if o == 0:
                        ada_aside("out1", g, 0, 2 * g + (4 * KT + 8))
                own.leave(p.iters)
            split_lo(ph["ffa"], 0, 2)
            dve.wait_ge(mod_done, 16 + 4)
            one_plus(2, 2, 4 * KT)
            residual(y1, 1, 2)
            split_lo(ph["ffa"], 0, 3)
            norm(1, 3, lambda k: gain[:, 2, one(k)], 3 * KT)

            def ffn(name, pair0, dst, first, a, b, t, with_ada=False):
                p = ph[name]
                for g in bodies(dve, p, first=p.opens):
                    own.enter(4 + 2 * with_ada, g, first=p.opens)
                    for i in range(4):
                        f = 4 * g + i
                        ahead(p, g, 2 * i)
                        evac(p, g, 2 * i, a[i % 2][:])
                        if with_ada and i % 2 == 0:
                            ada_aside(name, g, i, f + 5 * KT)
                        ahead(p, g, 2 * i + 1)
                        evac(p, g, 2 * i + 1, b[i % 2][:], own_use=True)
                        dve.wait_ge(f_tanh, f + (pair0 + 1))
                        own.step(stt(a[i % 2][:], t[i % 2][:], 1.0, a[i % 2][:], ADD, MUL))
                        tt(a[i % 2][:], a[i % 2][:], b[i % 2][:], MUL).then_inc(f_done, 1)
                        dve.wait_ge(f_hi, f + (pair0 + 1))
                        stt(dst[:, f + first, T:], a[i % 2][:], 0.5, dst[:, f + first, 0:T], MUL, SUB).then_inc(f_split, 1)
                    own.leave(1 if p.opens and opening(g) else p.iters - p.opens)

            ffn("ffa", 0, f1, 0, f1_a, f1_b, f1_t, with_ada=True)
            dve.wait_ge(mod_done, 16 + 4 + 8)
            gated(3, 3, 5 * KT)
            ffn("ffb", 16, f1, 16, f1_a, f1_b, f1_t)
            p = ph["down1"]
            for g in bodies(dve, p):
                for m in range(12):
                    ahead(p, g, m)
                    if m % 3 == 2:
                        evac(p, g, m // 3, y2[:, 4 * g + m // 3, :])
            split_lo(ph["att"], 0, 2)
            residual(y2, 3, 4)
            split_lo(ph["att"], 0, 3)

            norm(2, 5, lambda k: gains[:, 4, one(k)])
            dve.wait_ge(late_in, 16 * 9)
            dve.wait_ge(B0["hi"], 1)
            tt(wa_lo[:], wa_raw[:], wa_hi[:], SUB).then_inc(B0["lo"], 1)
            v.tensor_scalar(gla_norm[:], gla_norm[:], 0.5, None, MUL).then_inc(B0["norm"], 1)

            def gate_sum():
                dve.wait_ge(B0["half"], 1)
                tt(gla_ad[:], p_score[0:RANK, 0:T], gla_ad[:], ADD).then_inc(B0["ad"], 1)

            def gate_log():
                dve.wait_ge(B0["zb"], 1)
                stt(a_out[:], a_in[:], -1.0, a_in[:], MUL, ALU.max).then_inc(B0["abs"], 1)
                dve.wait_ge(B0["ln"], 1)
                own.step(stt(a_in[:], a_in[:], 0.0, a_out[:], ALU.min, SUB))
                for n in range(GLA_HEADS):
                    ins = v.tensor_tensor_scan(log_a[:, n, :], carry[:], a_in[:, n, :], 0.0, MUL, ADD)
                own.step(ins)
                ends = log_a[:].rearrange("p n (c t) -> p n c t", c=GLA_CHUNKS)[:, :, :, 63]
                v.tensor_scalar(a_last[:], ends, 1.0 / GLA_TAU, None, MUL).then_inc(B0["cum"], 1)

            def att_before(r, g, i, n):
                if r == 1:
                    dve.wait_ge(A["exp"], n)
                    own.step(v.reciprocal(sm[:, 3, :], sm[:, 2, :]))
                    for s in range(2):
                        ins = v.tensor_scalar(ex[:, s, :], ex[:, s, :], sm[:, 3, s:s + 1], None, MUL)
                    ins.then_inc(A["p"], 1)

            def att_after(r, g, i, n):
                if r == 0:
                    dve.wait_ge(A["scored"], n)
                    slope = slopes[:, one(4 * g + i - 1)]
                    own.step(stt(pre[:].rearrange("p s t -> p (s t)"), ago[:].rearrange("p s t -> p (s t)"), slope, p_score[:],
                                 MUL, ADD))
                    own.step(v.tensor_reduce(sm[:, 0, :], pre[:], AX_X, ALU.max))
                    v.tensor_scalar(sm[:, 1, :], sm[:, 0, :], -QK_SCALE, None, MUL).then_inc(A["max"], 1)
                elif r == 2:
                    dve.wait_ge(A["hi"], n)
                    done = o_att[:, 4 * g + i - 1, :]
                    tt(done[:, T:], p_o[:, 0:T], done[:, 0:T], SUB).then_inc(A["done"], 1)

            p = ph["att"]
            for g in bodies(dve, p, first=1):
                peeled = opening(g)
                own.enter(3 * (3 if peeled else 4) + 2 * peeled, g, first=1)
                for m in range(12):
                    i, r = divmod(m, 3)
                    prev = not (peeled and i == 0)
                    if prev:
                        att_before(r, g, i, 4 * g + i)
                    ahead(p, g, m)
                    evac(p, g, m, (att_q, att_k, att_v)[r][i % 2][:])
                    if prev:
                        att_after(r, g, i, 4 * g + i)
                    elif r == 0:
                        gate_sum()
                    elif r == 1:
                        gate_log()
                own.leave(1 if peeled else p.iters - 1)
            for r in range(3):
                att_before(r, p.iters, 0, HEADS)
                att_after(r, p.iters, 0, HEADS)

            dve.wait_ge(B0["decays"], 1)
            v.memset(k_dec_n[:], 0.0)
            v.memset(intra[:], 0.0).then_inc(B0["zero"], 1)

            def gla_before(r, g, i, n):
                if r == 5:
                    dve.wait_ge(B["std"], n)
                    own.step(v.reciprocal(go_rstd[:], go_std[:]))
                    own.step(tt(go[:], go[:], pair(go_rstd[:]), MUL))
                    tt(go[:], go[:], gr_act[:], MUL).then_inc(B["out"], 1)

            def gla_after(r, g, i, n):
                head = 2 * g + i - 1
                if r == 0:
                    dve.wait_ge(B["tanh"], n)
                    stt(gr_act[:], gr_act[:], 1.0, gr_t[:], ADD, MUL)
                    dve.wait_ge(B["scored"], n)
                    v.copy_predicated(intra[:].rearrange("p s t -> p (s t)"), causal[:].rearrange("p s t -> p (s t)"),
                                      p_score[:, 0:T]).then_inc(B["intra"], 1)
                elif r == 1:
                    dve.wait_ge(B["s1"], n)
                    own.step(stt(state[1][:], state[0][:], a_in[:, head, 127:128], p_y[:, T:], MUL, ADD))
                    stt(state[2][:], state[1][:], a_in[:, head, 191:192], p_z[:, T:], MUL, ADD).then_inc(B["states"], 1)
                elif r == 5:
                    dve.wait_ge(B["hi"], n)
                    for j in range(2):
                        done = o_gla[:, head, j, :]
                        ins = stt(done[:, T:], go[:, j, :], gla_norm[:, j:j + 1], done[:, 0:T], MUL, SUB)
                    ins.then_inc(B["done"], 1)

            p = ph["gla"]
            for g in bodies(dve, p, first=1):
                prev = [not opening(g), True]
                own.enter(3 * sum(prev), g, first=1)
                for m in range(12):
                    i, r = divmod(m, 6)
                    n = 2 * g + i
                    ahead(p, g, m)
                    if prev[i]:
                        gla_before(r, g, i, n)
                        if r == 2:
                            dve.wait_ge(B["turned"], n)
                    dst = (gq[:], gk[:], gv_t[:, 0, :], gv_t[:, 1, :], gr_t[:, 0, :], gr_t[:, 1, :])[r]
                    evac(p, g, m, dst, own_use=r == 1)
                    if r == 1:
                        stt(q_in[i][:], gq[:], QK_SCALE, a_in[:, n, :], MUL, MUL)
                        tt(k_in[:], gk[:], a_out[:, n, :], MUL)
                        tt(k_dec[:], gk[:], a_end[:, n, :], MUL).then_inc(B["qk"], 1)
                    if prev[i]:
                        gla_after(r, g, i, n)
                own.leave(1 if isinstance(g, int) else p.iters - 1)
            for r in range(6):
                gla_before(r, p.iters, 0, GLA_HEADS)
                gla_after(r, p.iters, 0, GLA_HEADS)

            own.step(v.memset(cp[:, 0:2], 0.0))
            p = ph["conv"]
            for g in bodies(dve, p):
                own.enter(4 * 4, g)
                for m in range(12):
                    ct, r = 4 * g + m // 3, m % 3
                    ahead(p, g, m)
                    evac(p, g, m, (cc, cu, cb)[r][:], own_use=r > 0)
                    if r == 1:
                        own.step(tt(cp[:, 2:], cc[:], cu[:], MUL))
                    elif r == 2:
                        own.step(v.tensor_scalar(cy[:], cp[:, 2:], conv_w[:, ct, 2:3], None, MUL))
                        own.step(stt(cy[:], cp[:, 1:T + 1], conv_w[:, ct, 1:2], cy[:], MUL, ADD))
                        own.step(stt(cy[:], cp[:, 0:T], conv_w[:, ct, 0:1], cy[:], MUL, ADD))
                        tt(cy[:], cy[:], cb[:], MUL).then_inc(cv_done, 1)
                        dve.wait_ge(cv_hi, ct + 1)
                        tt(y_conv[:, ct, T:], cy[:], y_conv[:, ct, 0:T], SUB).then_inc(cv_split, 1)
                own.leave(p.iters)

            p = ph["mrg0"]
            for g in bodies(dve, p, first=1):
                for m in range(4):
                    ahead(p, g, m)
                    if not (opening(g) and m < 2):
                        dve.wait_ge(t0_done, 4 * g + (m - 1))
                    evac(p, g, m, mg[m % 2][:])

            p = ph["mix"]
            dve.wait_ge(t0_done, KT)
            for g in bodies(dve, p):
                own.enter(2 * 2, g)
                for i in range(2):
                    d = 2 * g + i
                    for r in range(5):
                        if r in (0, 1, 2, 4):
                            ahead(p, g, 4 * i + min(r, 3))
                        evac(p, g, 5 * i + r, (mg + br)[r][:], own_use=r == 4)
                    dve.wait_ge(mt_done, d + 1)
                    for n, t in enumerate((t0[:, d, :], mg[0][:], mg[1][:])):
                        ins = stt(br[n][:], t, 1.0, br[n][:], ADD, MUL)
                    own.step(ins)
                    own.step(tt(br[0][:], br[0][:], br[1][:], ADD))
                    tt(br[0][:], br[0][:], br[2][:], ADD).then_inc(mx_done, 1)
                    mx = mixed[:, d, :]
                    dve.wait_ge(mx_hi, d + 1)
                    stt(mx[:, T:], br[0][:], 0.5, mx[:, 0:T], MUL, SUB).then_inc(mx_split, 1)
                own.leave(p.iters)

            def into_residual(name, y, updates, blocks, last=0):
                p = ph[name]
                for g in bodies(dve, p, last=last):
                    for m in range(4 * blocks):
                        ahead(p, g, m, last and isinstance(g, int))
                        if m % blocks == blocks - 1:
                            o = m // blocks
                            d = 4 * g + o
                            evac(p, g, o, y[:], own_use=True)
                            tt(x[:, d, :], x[:, d, :], y[:], ADD).then_inc(y_done, 1)
                            dve.wait_ge(y_done, d + (16 * updates + 1))

            into_residual("out2", y_out, 2, 1)
            split_lo(ph["ff2"], 0, 2)
            norm(3, 6, lambda k: gains[:, 5, one(k)])
            split_lo(ph["ff2"], 0, 3)
            ffn("ff2", FF, f2, 0, f2_a, f2_b, f2_t)
            into_residual("down2", y_down, 3, 3, last=1)

            inverse_std(7)
            for kt in range(KT):
                stt(x[:, kt, :], x[:, kt, :], gains[:, 6, kt:kt + 1], rstd[:], MUL, MUL).then_inc(out_ready, 1)

        @block.gpsimd
        def _(pool):
            tt = nc.gpsimd.tensor_tensor
            own = Own(pool, pool_own)

            def clear_sum(stage):
                if stage:
                    pool.wait_ge(std_done, stage)
                own.step(nc.gpsimd.memset(sq_sum[:], 0.0))

            def add_square(count, b):
                pool.wait_ge(sq_done, count)
                tt(sq_sum[:], sq_sum[:], tile[b][:], ALU.add).then_inc(sq_used, 1)
                pool.wait_ge(sq_used, count)

            def sum_squares(stage):
                clear_sum(stage)
                with pool.Fori(0, KT // 4) as q:
                    for b in range(4):
                        add_square(4 * q + (KT * stage + b + 1), b % 2)

            def ada_aside(name, g, i):
                buffer, k = aside[name][i % 2], i % 2
                pool.wait_ge(aside_in[k], 16 * ph[name].aside_count(g, i))
                tt(buffer[:], buffer[:], c_act[:], ALU.mult).then_inc(aside_mul[k], 1)

            RUN = 16
            up = [(d, 2 * d - 1, 2 * d) for d in (2, 4, 8)]
            across = [(d, d + RUN - 1, RUN) for d in (16, 32, 64, 128)]
            down = [(d, 3 * d - 1, 2 * d) for d in (8, 4, 2)]
            levels = up + across + down
            with pool.Fori(0, S5_TILES // 2) as g:
                own.enter(2 * (3 * len(levels) - 1), g)
                for i in range(2):
                    pool.wait_ge(x_ready, 2 * g + (i + 1))
                    xs = s5_x[i]
                    for level, (back, first, stride) in enumerate(levels):
                        n = (T - 1 - first) // stride + 1
                        end = first + stride * (n - 1) + 1
                        to = slice(first, end, stride)
                        frm = slice(first - back, end - back, stride)
                        k = back.bit_length() - 1
                        by = s5_now[i][:, 4 * k:4 * k + 4].rearrange("p (a c) -> p a c", c=2)
                        prod = s5_prod[:, :, :, 0:n]
                        own.step(tt(prod, xs[:, :, frm].unsqueeze(1).to_broadcast([P, 2, 2, n]),
                                    by.unsqueeze(3).to_broadcast([P, 2, 2, n]), ALU.mult))
                        own.step(tt(xs[:, :, to], prod[:, :, 0, :], xs[:, :, to], ALU.add))
                        ins = tt(xs[:, :, to], prod[:, :, 1, :], xs[:, :, to], ALU.add)
                        if level == len(levels) - 1:
                            ins.then_inc(scan_core, 1)
                        else:
                            own.step(ins)
                    pool.wait_ge(scan_core, 2 * g + (i + 1))
                own.leave(S5_TILES // 2)
            for g in bodies(pool, ph["glu"]):
                for i in range(4):
                    ada_aside("glu", g, i)
            clear_sum(1)
            for g in bodies(pool, ph["out1"]):
                for o in range(4):
                    if o == 3:
                        ada_aside("out1", g, 1)
                    add_square(4 * g + (KT + o + 1), o % 2)
            for g in bodies(pool, ph["ffa"]):
                for i in (1, 3):
                    ada_aside("ffa", g, i)
            for stage in (3, 5, 6):
                sum_squares(stage)


def weight_tiles(w, col):
    return w[:, col:col + P].reshape(-1, P, P).transpose(1, 0, 2)


def columns(v):
    return v.reshape(-1, P).T


def layouts(i):
    import numpy as np

    ph = schedule()
    a = {k: np.asarray(v) for k, v in i.items()}
    out = {}

    def put(name, blocks):
        p = ph[name]
        flat = np.empty((p.iters, p.words), np.float32)
        it = iter(blocks)
        for g in range(p.iters):
            for off, (kind, n) in zip(p.offsets, p.blocks):
                flat[g, off:off + n * P * P] = next(ada if kind == ADA or p.summed else it).reshape(-1)
        assert next(it, None) is None
        out["w_" + name] = flat

    ada = iter(a["w_ada"][0].T.reshape(96, P, D))
    w_in, w2 = a["w_in"][0], a["w_in_2"][0]
    Q, K, V, G, U, GR, GS = 0, 1024, 2048, 4096, 6144, 7168, 9216
    put("ada", iter(()))
    put("u", (weight_tiles(w_in, U + P * t) for t in range(HALF)))
    put("heads", (weight_tiles(w_in, c) for h in range(HEADS)
                  for c in (Q + P * h, K + P * h, V + 2 * P * h, V + 2 * P * h + P, G + 2 * P * h, G + 2 * P * h + P)))
    put("ret", (t for d in range(KT) for t in (weight_tiles(w_in, GR + P * d), weight_tiles(a["w_ret_out"][0], P * d))))
    glu = a["w_s5_glu"][0]
    put("glu", (t for d in range(KT) for t in (weight_tiles(w_in, GS + P * d),
                                               np.concatenate([weight_tiles(glu, P * d), weight_tiles(glu, D + P * d)], 1))))
    put("out1", (weight_tiles(a["w_out"][0], P * d) for d in range(KT)))
    ff = a["w_ffn_in"][0]
    pair1 = lambda f: (weight_tiles(ff, P * f), weight_tiles(ff, FF * P + P * f))
    put("ffa", (t for f in range(KT) for t in pair1(f)))
    put("ffb", (t for f in range(KT, FF) for t in pair1(f)))

    def down(w):
        for d in range(KT):
            t = weight_tiles(w, P * d)
            yield t[:, 0:16]
            yield t[:, 16:32]
            yield t[:, 32:44]

    put("down1", down(a["w_ffn_out"][0]))
    A3, QG, KG, VG, RG, AD, BG, CG, UC, MG = 0, 3072, 3584, 4096, 5120, 6144, 6160, 7184, 8208, 9232
    put("att", (weight_tiles(w2, A3 + 1024 * r + P * h) for h in range(HEADS) for r in range(3)))
    put("gla", (weight_tiles(w2, c) for h in range(GLA_HEADS)
                for c in (QG + P * h, KG + P * h, VG + 2 * P * h, VG + 2 * P * h + P, RG + 2 * P * h, RG + 2 * P * h + P)))
    put("conv", (weight_tiles(w2, c + P * t) for t in range(HALF) for c in (CG, UC, BG)))
    put("mrg0", (weight_tiles(w2, MG + P * d) for d in range(KT)))

    def mix():
        ba, bg, bc = a["w_br_attn_2"][0], a["w_br_gla_2"][0], a["w_br_conv_2"][0]
        for d in range(KT):
            yield weight_tiles(w2, MG + D + P * d)
            yield weight_tiles(w2, MG + 2 * D + P * d)
            yield np.concatenate([weight_tiles(ba, P * d), weight_tiles(bg, P * d)], 1)
            yield weight_tiles(bc, P * d)

    put("mix", mix())
    put("out2", (weight_tiles(a["w_out_2"][0], P * d) for d in range(KT)))
    put("ff2", (t for f in range(FF) for t in (weight_tiles(a["w_ffn_gate_2"][0], P * f), weight_tiles(a["w_ffn_up_2"][0], P * f))))
    put("down2", down(a["w_ffn_down_2"][0]))

    out["x_t"] = a["x"][0].T.reshape(KT, P, T).transpose(1, 0, 2)
    out["c_rows"] = np.broadcast_to(a["c"], (P, D))
    out["b_ada_c"] = columns(a["b_ada"][0])
    out["gains"] = np.stack([columns(a["norm_gains"][0, n]) for n in range(4)]
                            + [columns(a["norm1_w_2"][0]), columns(a["norm2_w_2"][0]), columns(a["final_norm_w_2"])], 1)

    def states(v):
        return v.reshape(S5_TILES, P).T

    out["s5_a"] = np.stack([states(a["ssm_a_re"][0]), states(a["ssm_a_im"][0]),
                            states(np.repeat(a["ssm_log_dt"][0], 64))], 1)
    b = np.zeros((S5_TILES, P, 2, P), np.float32)
    c = np.zeros((S5_TILES, P, 2, P), np.float32)
    for n, (bb, cc) in enumerate(((a["ssm_b_re"][0], a["ssm_c_re"][0]), (a["ssm_b_im"][0], a["ssm_c_im"][0]))):
        for g in range(2 * S5_TILES):
            i, e = g // 2, g % 2
            ch = 32 * (i % 4) + 16 * e
            b[i, ch:ch + 16, n, 64 * e:64 * e + 64] = bb[g].T
            c[i, 64 * e:64 * e + 64, n, ch:ch + 16] = cc[g].T
    out["s5_b"], out["s5_c"] = b, c
    out["s5_d"] = columns(a["ssm_d"][0].reshape(-1))

    out["gla_down"] = w2[:, AD:AD + RANK].reshape(KT, P, RANK).transpose(1, 0, 2)
    out["gla_up"] = a["gla_w_up_2"][0]
    out["gla_b"] = columns(a["gla_b_2"][0])
    out["gla_norm"] = columns(a["gla_norm_w_2"][0])
    out["conv_w"] = np.stack([columns(a["conv_w_2"][0, n]) for n in range(3)], 2)

    f32 = np.float32
    pos = np.arange(T, dtype=f32)
    inv = (f32(10000.0) ** (-np.arange(64, dtype=f32) * f32(2.0 / 128))).astype(f32)
    ang = pos[None, :] * inv[:, None]
    cos, sin = np.cos(ang).astype(f32), np.sin(ang).astype(f32)
    out["rope"] = np.stack([np.concatenate([cos, cos]), np.concatenate([sin, -sin])], 1)
    s, t = np.arange(P)[:, None], np.arange(T)[None, :]
    lag = np.where(t >= s, t - s, 1e8).astype(f32)
    out["lag"] = lag
    log_g = np.log1p(-np.exp2(-5.0 - np.arange(HEADS, dtype=f32))).astype(f32)
    out["log_g"] = np.broadcast_to(log_g, (P, HEADS))
    key = np.arange(T)[None, :]
    out["ago"] = np.stack([np.where(key <= s + P * n, key - (s + P * n), -1e30) for n in range(2)], 1).astype(f32)
    out["slopes"] = np.broadcast_to((2.0 ** -np.arange(1.0, HEADS + 1) / QK_SCALE).astype(f32), (P, HEADS))
    out["chunk_causal"] = np.broadcast_to(((s // 64 == t[:, 0:P] // 64) & (s <= t[:, 0:P]))[:, None], (P, 2, P)).astype(np.int32)
    out["chunk_carry"] = np.broadcast_to((t % 64 != 0), (P, T)).astype(f32)
    out["identity"] = np.eye(P, dtype=f32)
    return {k: np.ascontiguousarray(v) for k, v in out.items()}


def kernel(**inputs):
    import numpy as np
    from concourse import bacc
    from concourse.bass_utils import run_bass_kernel_spmd

    nc = bacc.Bacc("TRN2", target_bir_lowering=False, num_devices=1, dynamic_dma_scratch_size=1024)
    arrays = layouts(inputs)
    dram = {k: nc.dram_tensor(k, v.shape, mybir.dt.from_np(v.dtype), kind="ExternalInput").ap() for k, v in arrays.items()}
    out = nc.dram_tensor("out_t", (KT, P, T), F32, kind="ExternalOutput").ap()
    program(nc, dram, out)
    r = run_bass_kernel_spmd(nc, [arrays], core_ids=[0])
    return np.ascontiguousarray(r.results[0]["out_t"].reshape(D, T).T)[None]
```
